# Optimizing a Trainium2 kernel written in Bass

```python
import jax, jax.numpy as jnp
from jax import lax
import numpy as np

D_MODEL = 1024
BATCH = 1
SEQ = 512
DEPTH = 2

HEAD_DIM = 128
N_Q_HEADS = D_MODEL // HEAD_DIM
N_KV_HEADS = N_Q_HEADS // 4
W_ATT = N_Q_HEADS * HEAD_DIM
W_KV = N_KV_HEADS * HEAD_DIM
W_SC = D_MODEL
SC_WIDTH = 3
W_CF = D_MODEL
CF_WIDTH = 31
GRID_W = 64
Q_BLOCK = 128
ROPE_THETA = 10000.0
RMS_EPS = 1e-6
LN_EPS = 1e-5
SPLITS = (W_SC, W_SC, W_SC, W_SC,
          W_ATT, W_KV, W_KV, W_ATT,
          W_CF, W_CF, W_CF,
          D_MODEL, D_MODEL, D_MODEL)
P_IN = sum(SPLITS)

kernel_name = "hybrid_conv_gqa_conformer_encoder"

def rms_norm(x, g):
    x32 = x.astype(jnp.float32)
    y = x32 * lax.rsqrt(jnp.mean(x32 * x32, axis=-1, keepdims=True) + RMS_EPS)
    return (y * g.astype(jnp.float32)).astype(x.dtype)

def layer_norm(x, g, b):
    x32 = x.astype(jnp.float32)
    mu = jnp.mean(x32, axis=-1, keepdims=True)
    xc = x32 - mu
    y = xc * lax.rsqrt(jnp.mean(xc * xc, axis=-1, keepdims=True) + LN_EPS)
    return (y * g.astype(jnp.float32) + b.astype(jnp.float32)).astype(x.dtype)

def depthwise_conv(x, w):
    k = w.shape[0]
    return lax.conv_general_dilated(
        x, w[:, None, :], window_strides=(1,), padding=[(k // 2, k // 2)],
        dimension_numbers=("NWC", "WIO", "NWC"), feature_group_count=x.shape[-1])

def axial_rope_tables(seq_len):
    n_rows = seq_len // GRID_W
    rows = jnp.repeat(jnp.arange(n_rows), GRID_W)
    cols = jnp.tile(jnp.arange(GRID_W), n_rows)
    n_freq = HEAD_DIM // 4
    inv_freq = ROPE_THETA ** (-jnp.arange(n_freq, dtype=jnp.float32) / n_freq)
    pos = jnp.stack([rows, cols], axis=-1).astype(jnp.float32)
    ang = pos[:, :, None] * inv_freq
    return jnp.cos(ang), jnp.sin(ang)

def apply_axial_rope(x, cos, sin):
    b, s, h, d = x.shape
    n_freq = d // 4
    xr = x.astype(jnp.float32).reshape(b, s, h, 2, 2, n_freq)
    x1, x2 = xr[..., 0, :], xr[..., 1, :]
    c = cos[None, :, None]
    sn = sin[None, :, None]
    out = jnp.stack([x1 * c - x2 * sn, x2 * c + x1 * sn], axis=-2)
    return out.reshape(b, s, h, d).astype(x.dtype)

def block_gqa_attention(q, k, v):
    b, s, hq, hd = q.shape
    hkv = k.shape[2]
    g = hq // hkv
    nb = s // Q_BLOCK
    qb = q.reshape(b, nb, Q_BLOCK, hkv, g, hd).transpose(1, 0, 2, 3, 4, 5)
    scale = hd ** -0.5

    def one_block(qi):
        sc = jnp.einsum("bqkgd,bskd->bkgqs", qi, k).astype(jnp.float32) * scale
        p = jax.nn.softmax(sc, axis=-1).astype(v.dtype)
        return jnp.einsum("bkgqs,bskd->bqkgd", p, v)

    o = lax.map(one_block, qb)
    return o.transpose(1, 0, 2, 3, 4, 5).reshape(b, s, hq * hd)

def hybrid_layer(x, cos, sin, norm_pre, norm_post, w_in, conv_a_w, q_norm, k_norm,
                 conv_c_w, conv_c_b, ln_c_g, ln_c_b, w_out_a, w_out_b, w_out_c, w_o):
    b, s, _ = x.shape
    h = rms_norm(x, norm_pre)
    proj = h @ w_in
    offsets = []
    acc = 0
    for w in SPLITS[:-1]:
        acc += w
        offsets.append(acc)
    (a_b, a_c, a_x, a_g, q, k, v, b_g, c_u, c_v, c_g,
     m_a, m_b, m_c) = jnp.split(proj, offsets, axis=-1)

    ya = a_b * depthwise_conv(a_c * a_x, conv_a_w)
    ya = (ya * jax.nn.silu(a_g)) @ w_out_a

    q = apply_axial_rope(rms_norm(q.reshape(b, s, N_Q_HEADS, HEAD_DIM), q_norm), cos, sin)
    k = apply_axial_rope(rms_norm(k.reshape(b, s, N_KV_HEADS, HEAD_DIM), k_norm), cos, sin)
    v = v.reshape(b, s, N_KV_HEADS, HEAD_DIM)
    yb = (block_gqa_attention(q, k, v) * jax.nn.silu(b_g)) @ w_out_b

    u = c_u * jax.nn.sigmoid(c_v)
    u = depthwise_conv(u, conv_c_w) + conv_c_b
    u = jax.nn.silu(layer_norm(u, ln_c_g, ln_c_b))
    yc = (u * jax.nn.silu(c_g)) @ w_out_c

    y = jax.nn.sigmoid(m_a) * ya + jax.nn.sigmoid(m_b) * yb + jax.nn.sigmoid(m_c) * yc
    return x + rms_norm(y @ w_o, norm_post)

def setup_inputs(seed: int = 0) -> dict:
    key = jax.random.key(seed)
    ks = jax.random.split(key, 16)
    f32 = jnp.float32
    L, D = DEPTH, D_MODEL

    def nrm(k, shape, scale):
        return jax.random.normal(k, shape, f32) * scale

    return {
        "x": nrm(ks[0], (BATCH, SEQ, D), 1.0),
        "norm_pre": 1.0 + nrm(ks[1], (L, D), 0.05),
        "norm_post": 1.0 + nrm(ks[2], (L, D), 0.05),
        "w_in": nrm(ks[3], (L, D, P_IN), D ** -0.5),
        "conv_a_w": nrm(ks[4], (L, SC_WIDTH, W_SC), SC_WIDTH ** -0.5),
        "q_norm": 1.0 + nrm(ks[5], (L, HEAD_DIM), 0.05),
        "k_norm": 1.0 + nrm(ks[6], (L, HEAD_DIM), 0.05),
        "conv_c_w": nrm(ks[7], (L, CF_WIDTH, W_CF), CF_WIDTH ** -0.5),
        "conv_c_b": nrm(ks[8], (L, W_CF), 0.02),
        "ln_c_g": 1.0 + nrm(ks[9], (L, W_CF), 0.05),
        "ln_c_b": nrm(ks[10], (L, W_CF), 0.02),
        "w_out_a": nrm(ks[11], (L, W_SC, D), W_SC ** -0.5),
        "w_out_b": nrm(ks[12], (L, W_ATT, D), W_ATT ** -0.5),
        "w_out_c": nrm(ks[13], (L, W_CF, D), W_CF ** -0.5),
        "w_o": nrm(ks[14], (L, D, D), D ** -0.5),
    }

def reference(x, norm_pre, norm_post, w_in, conv_a_w, q_norm, k_norm, conv_c_w, conv_c_b,
              ln_c_g, ln_c_b, w_out_a, w_out_b, w_out_c, w_o):
    cos, sin = axial_rope_tables(x.shape[1])
    for l in range(DEPTH):
        x = hybrid_layer(x, cos, sin, norm_pre[l], norm_post[l], w_in[l], conv_a_w[l],
                         q_norm[l], k_norm[l], conv_c_w[l], conv_c_b[l], ln_c_g[l], ln_c_b[l],
                         w_out_a[l], w_out_b[l], w_out_c[l], w_o[l])
    return x


_drawn_inputs = setup_inputs


def setup_inputs(seed=0):
    import zlib

    import numpy as np

    out = dict(_drawn_inputs(seed))
    spreads = {}
    factors = {'q_norm': 8.0, 'k_norm': 8.0, 'ln_c_b': 4.606}
    for name, (base, spread) in spreads.items():
        noise = np.random.default_rng([zlib.crc32(name.encode()), seed]).standard_normal(out[name].shape)
        drawn = base * np.exp(spread * noise) if base else spread * noise
        out[name] = __import__('jax').numpy.asarray(drawn.astype(out[name].dtype))
    for name, factor in factors.items():
        out[name] = (out[name] * factor).astype(out[name].dtype)
    return out
```

```python
from contextlib import ExitStack

import numpy as np

import concourse.bass as bass
from concourse import mybir
from concourse.alu_op_type import AluOpType as ALU

F32 = mybir.dt.float32
F32R = mybir.dt.float32r
ACT = mybir.ActivationFunctionType
AX_X = mybir.AxisListType.X

P = 128
D = 1024
SEQ = 512
DEPTH = 2
KC = D // P
TB = SEQ // P
HEADS = KC
KV_HEADS = 2
GROUP = HEADS // KV_HEADS
TAPS_A, TAPS_C = 3, 31
PAD_A, PAD_C = TAPS_A // 2, TAPS_C // 2
RMS_EPS, LN_EPS = 1e-6, 1e-5
SCALE = float(P) ** -0.5
GRID_W, THETA = 64, 10000.0

SPLIT_NAMES = ("a_b", "a_c", "a_x", "a_g", "q", "k", "v", "b_g", "c_u", "c_v", "c_g", "m_a", "m_b", "m_c")
SPLIT_BLOCKS = (KC, KC, KC, KC, HEADS, KV_HEADS, KV_HEADS, KC, KC, KC, KC, KC, KC, KC)
FIRST_BLOCK = {n: sum(SPLIT_BLOCKS[:i]) for i, n in enumerate(SPLIT_NAMES)}
UNIT_TILES = ("q", "a_c", "a_x", "a_b", "a_g", "b_g", "c_v", "c_u")
UT = len(UNIT_TILES)

GROUP_SLABS = 2 + GROUP * UT
GROUP_USES = TB + GROUP * UT
SLAB_A = KV_HEADS * GROUP_SLABS
USE_A = KV_HEADS * GROUP_USES
SLAB_B, USE_B = SLAB_A + 2 * KC, USE_A + 2 * KC
SLAB_G, USE_G = SLAB_B + 2 * KC, USE_B + 2 * KC
SLAB_C, USE_C = SLAB_G + KC, USE_G + KC
SLAB_O, USE_O = SLAB_C + 2 * KC, USE_C + 2 * KC
QUARTERS = 4
LAYER_SLABS = SLAB_O + KC
LAYER_USES = USE_O + QUARTERS * TB
BANKS = 4
LAYER_TURNS = LAYER_USES // BANKS

PC_C = 0
PC_BIAS = PC_C + (KC + 1) * TAPS_C
PC_A = PC_BIAS + KC + 1
PC_LNG = PC_A + KC * TAPS_A
PC_LNB = PC_LNG + KC
PC_GQ = PC_LNB + KC
PC_GK = PC_GQ + 1
PC_N = PC_GK + 1


def slab_order():
    order = []
    for g in range(KV_HEADS):
        order += [("w_in", FIRST_BLOCK["k"] + g), ("w_in", FIRST_BLOCK["v"] + g)]
        for i in range(GROUP):
            order += [("w_in", FIRST_BLOCK[n] + g * GROUP + i) for n in UNIT_TILES]
    for gate, out in (("m_a", "w_out_a"), ("m_b", "w_out_b")):
        for j in range(KC):
            order += [("w_in", FIRST_BLOCK[gate] + j), (out, j)]
    order += [("w_in", FIRST_BLOCK["c_g"] + j) for j in range(KC)]
    for j in range(KC):
        order += [("w_in", FIRST_BLOCK["m_c"] + j), ("w_out_c", j)]
    order += [("w_o", j) for j in range(KC)]
    assert len(order) == LAYER_SLABS
    return order


def encoder_kernel(nc, x, slabs, params, pre_gain, post_gain, ident, rot, cos, sin, residual, out):
    with ExitStack() as ctx:
        def sb(name, shape, dt=F32, where=ctx):
            return where.enter_context(nc.sbuf_tensor(name, shape, dt))

        def sem(name):
            return ctx.enter_context(nc.semaphore(name))

        h_hi, h_lo = sb("h_hi", [P, KC, SEQ], F32R), sb("h_lo", [P, KC, SEQ], F32R)
        with ExitStack() as p1_time:
            p1_hi, p1_lo = (sb(n, [P, KC, SEQ], F32R, p1_time) for n in ("p1_hi", "p1_lo"))
        alt_hi, alt_lo = sb("alt_hi", [P, 2, KC, P], F32R), sb("alt_lo", [P, 2, KC, P], F32R)
        sb("p1_rest", [P, KC, SEQ])
        p2_hi, p2_lo = sb("p2_hi", [P, KC, SEQ], F32R), sb("p2_lo", [P, KC, SEQ], F32R)
        cc = sb("cc", [P, KC + 1, SEQ])
        xres = cc[:, 1:KC + 1, :].rearrange("p (t a) n -> p t (a n)", t=TB)
        raw = sb("raw", [P, 2, KC, P])
        w_hi, w_lo = sb("w_hi", [P, 2, KC, P], F32R), sb("w_lo", [P, 2, KC, P], F32R)
        with ExitStack() as attention_time:
            k_hi, k_lo = (sb(n, [P, SEQ], F32R, attention_time) for n in ("k_hi", "k_lo"))
            v_hi, v_lo = (sb(n, [P, TB, P], F32R, attention_time) for n in ("v_hi", "v_lo"))
            probs = sb("probs", [P, TB, SEQ], F32, attention_time)
            pt_hi, pt_lo = (sb(n, [P, 2, SEQ], F32R, attention_time) for n in ("pt_hi", "pt_lo"))
            g_hi, g_lo = (sb(n, [P, SEQ], F32R, attention_time) for n in ("g_hi", "g_lo"))
            r_hi, r_lo = (sb(n, [P, SEQ], F32R, attention_time) for n in ("r_hi", "r_lo"))
            rope1, rope2 = (sb(n, [P, SEQ], F32, attention_time) for n in ("rope1", "rope2"))
        k_raw = probs[:, 0, :].rearrange("p (t n) -> p t n", t=TB)
        k_junk = probs[:, 1, 0:P]
        with ExitStack() as y_time:
            y = sb("y", [P, KC, SEQ], F32, y_time)
            sq = sb("sq", [P, KC, SEQ], F32, y_time)
        xn = sb("xn", [P, 2, D])
        junk = sb("junk", [P, 2 * D])
        yo = sb("yo", [P, TB, D])
        rot_f = sb("attention_rest", [P, 2 * SEQ])[:, 0:P]
        cos_sb, sin_sb = sb("cos_sb", [P, SEQ]), sb("sin_sb", [P, SEQ])
        upad = sb("upad", [P, SEQ + 2 * PAD_C])
        axpad = sb("axpad", [P, SEQ + 2 * PAD_A])
        gpre, gpost = sb("gpre", [P, D]), sb("gpost", [P, D])
        acc1 = sb("acc1", [P, SEQ])
        gate = sb("gate", [P, SEQ])
        ac_sb = sb("ac_sb", [P, SEQ])
        ca = sb("ca", [P, 2, SEQ])
        val = sb("val", [P, SEQ])
        bval = sb("bval", [P, SEQ])
        par = sb("par", [P, PC_N])
        ctap, atap, cbias = sb("ctap", [P, TAPS_C]), sb("atap", [P, TAPS_A]), sb("cbias", [P, 1])
        ident_sb, rot_r = sb("ident_sb", [P, P]), sb("rot_r", [P, P], F32R)
        mean_w = sb("mean_w", [P, P])
        ones = sb("ones", [P, 1])
        ln_eps = sb("ln_eps", [P, 1])
        half_neg = sb("half_neg", [P, TB])
        ss_x, ms_x, rx = (sb(n, [P, TB]) for n in ("ss_x", "ms_x", "rx"))
        ss_k, ms_k, rk = (sb(n, [P, TB]) for n in ("ss_k", "ms_k", "rk"))
        ms_q, rq, srq = (sb(n, [P, TB]) for n in ("ms_q", "rq", "srq"))
        ss_o, so, ms_o, ro = sb("ss_o", [P, TB, QUARTERS]), sb("so", [P, TB]), sb("ms_o", [P, TB]), sb("ro", [P, TB])
        mx, nb, rs, ri = (sb(n, [P, TB]) for n in ("mx", "nb", "rs", "ri"))

        bank = [ctx.enter_context(nc.psum_tensor(f"bank{i}", [P, SEQ], F32)) for i in range(BANKS)]
        ps_s, ps_t, ps_o, ps_c = (ctx.enter_context(nc.psum_tensor(n, [P, SEQ], F32)) for n in ("ps_s", "ps_t", "ps_o", "ps_c"))

        const_ld, saved, store = sem("const_ld"), sem("saved"), sem("store")
        xr_ld = [sem(f"xr_ld{t}") for t in range(TB)]
        pre_ld, post_ld = sem("pre_ld"), sem("post_ld")
        slab_ld = [sem(f"slab_ld{i}") for i in range(2)]
        hi_ready, lo_ready = sem("hi_ready"), sem("lo_ready")
        mm_done = sem("mm_done")
        taken = [sem(f"taken{i}") for i in range(BANKS)]
        setup = sem("setup")
        rot_ready, par_ld, taps_ready = sem("rot_ready"), sem("par_ld"), sem("taps_ready")
        x_ready, x_sq, x_ms, x_r, xn_ready, x_tr, h_hi_ready, h_lo_ready = (
            sem(n) for n in ("x_ready", "x_sq", "x_ms", "x_r", "xn_ready", "x_tr", "h_hi_ready", "h_lo_ready"))
        k_sq, k_copied, v_hi_ready, k_ms, k_r, k_norm, k_tr = (
            sem(n) for n in ("k_sq", "k_copied", "v_hi_ready", "k_ms", "k_r", "k_norm", "k_tr"))
        g_hi_ready, g_lo_ready, rope1_ready, rot_done, rope2_ready, roped, r_hi_ready, r_lo_ready = (
            sem(n) for n in ("g_hi_ready", "g_lo_ready", "rope1_ready", "rot_done", "rope2_ready", "roped", "r_hi_ready", "r_lo_ready"))
        q_sq, q_ss, q_ms, q_r, q_sr = (sem(n) for n in ("q_sq", "q_ss", "q_ms", "q_r", "q_sr"))
        s_done, s_max, s_nb, s_exp, s_ri, p_ready = (sem(n) for n in ("s_done", "s_max", "s_nb", "s_exp", "s_ri", "p_ready"))
        pt_tr, pt_hi_ready, pt_lo_ready, pv_done = (sem(n) for n in ("pt_tr", "pt_hi_ready", "pt_lo_ready", "pv_done"))
        b_tanh, b_val, b_hi, b_lo = (sem(n) for n in ("b_tanh", "b_val", "b_hi", "b_lo"))
        a_conv, a_tanh, a_val, a_hi, a_lo = (
            sem(n) for n in ("a_conv", "a_tanh", "a_val", "a_hi", "a_lo"))
        c_step, c_ready = sem("c_step"), sem("c_ready")
        m_tanh, m_val, y_ready, y_hi, y_lo = (sem(n) for n in ("m_tanh", "m_val", "y_ready", "y_hi", "y_lo"))
        ln_mean, ln_xc, ln_sq, ln_var, ln_sd, ln_r = (sem(n) for n in ("ln_mean", "ln_xc", "ln_sq", "ln_var", "ln_sd", "ln_r"))
        n_z, n_n, n_t, n_s, g_t, n_v, n_hi, n_lo = (
            sem(n) for n in ("n_z", "n_n", "n_t", "n_s", "g_t", "n_v", "n_hi", "n_lo"))
        o_sq, o_ss, o_ms, o_r, o_scaled = (sem(n) for n in ("o_sq", "o_ss", "o_ms", "o_r", "o_scaled"))

        def free_at(turns, b):
            return turns + b // BANKS + 1

        def taken_at(turns, b):
            return turns + b // BANKS + 2

        block = ctx.enter_context(nc.Block())

        @block.sync
        def _(sp):
            with sp.Fori(0, DEPTH * LAYER_SLABS // 2) as n2:
                for s in range(2):
                    sp.wait_ge(lo_ready, n2 * 2 + s + 1)
                    sp.dma_start(raw[:, s, :, :], slabs[n2, s]).then_inc(slab_ld[s], 16)

        @block.gpsimd
        def _(pool):
            pool.memset(ones[:], 1.0).then_inc(setup, 1)
            pool.memset(mean_w[:], 1.0 / D).then_inc(setup, 1)
            pool.memset(half_neg[:], -0.5).then_inc(setup, 1)
            pool.memset(ln_eps[:], LN_EPS).then_inc(setup, 1)
            pool.memset(upad[:], 0.0).then_inc(setup, 1)
            pool.memset(axpad[:], 0.0).then_inc(setup, 1)
            pool.memset(rs[:, 0:1], 0.0).then_inc(lo_ready, 2)
            pool.memset(rs[:, 1:2], 0.0).then_inc(mm_done, 2)
            pool.memset(rs[:, 2:3], 0.0).then_inc(c_ready, 1)
            for b in range(BANKS):
                pool.memset(mx[:, b:b + 1], 0.0).then_inc(taken[b], 1)
            pool.wait_ge(setup, 6)

            def lo(base, s, hi_to=w_hi, lo_to=w_lo):
                pool.wait_ge(hi_ready, base + s + 1)
                pool.tensor_tensor(lo_to[:, s % 2], raw[:, s % 2], hi_to[:, s % 2].bitcast(F32), ALU.subtract)\
                    .then_inc(lo_ready, 1)

            def power(ready, value, out, ms, done):
                pool.wait_ge(ready, value)
                pool.tensor_tensor(out, ms, half_neg[:, 0:out.shape[1]], ALU.pow).then_inc(done, 1)

            with pool.Fori(0, DEPTH) as l:
                for t in range(TB):
                    if t == 2:
                        for s in range(2):
                            lo(l * LAYER_SLABS, s)
                    power(x_ms, l * TB + t + 1, rx[:, t:t + 1], ms_x[:, t:t + 1], x_r)
                with pool.Fori(0, KV_HEADS) as g:
                    for s in range(2):
                        lo(l * LAYER_SLABS + g * GROUP_SLABS + 2, s)
                    power(k_ms, l * KV_HEADS + g + 1, rk[:], ms_k[:], k_r)
                    with pool.Fori(0, GROUP) as i:
                        base = l * LAYER_SLABS + g * GROUP_SLABS + i * UT + 2
                        u = l * HEADS + g * GROUP + i
                        for s in range(2, UT + 2):
                            lo(base, s)
                            if s == 2:
                                power(q_ms, u + 1, rq[:], ms_q[:], q_r)
                with pool.Fori(0, (SLAB_O - SLAB_A) // 2) as j:
                    for s in range(2):
                        lo(l * LAYER_SLABS + SLAB_A + 2 + j * 2, s)
                for q in range(1, QUARTERS):
                    for s in range(2):
                        hl = (w_hi, w_lo) if q % 2 == 0 else (alt_hi, alt_lo)
                        lo(l * LAYER_SLABS + SLAB_O + 2 * q, s, *hl)
                for t in range(TB):
                    power(o_ms, l * TB + t + 1, ro[:, t:t + 1], ms_o[:, t:t + 1], o_r)

        @block.scalar
        def _(act):
            for t in range(TB):
                act.dma_start(xres[:, t, :], x[t * P:(t + 1) * P, :]).then_inc(xr_ld[t], 16)
            act.dma_start(gpre[:], pre_gain[0].broadcast_to((P, D))).then_inc(pre_ld, 16)
            act.dma_start(ident_sb[:], ident).then_inc(const_ld, 16)
            act.dma_start(rot_f, rot).then_inc(const_ld, 16)
            act.dma_start(cos_sb[:], cos).then_inc(const_ld, 16)
            act.dma_start(sin_sb[:], sin).then_inc(const_ld, 16)
            act.dma_start(par[:], params[0]).then_inc(par_ld, 16)
            act.wait_ge(const_ld, 4 * 16)
            act.activation(rot_r[:], rot_f, ACT.Copy).then_inc(rot_ready, 1)

            def hi(base, s, use, hi_to=w_hi):
                act.wait_ge(slab_ld[s % 2], base * 8 + (s // 2 + 1) * 16)
                act.wait_ge(mm_done, use + (s - 1))
                act.activation(hi_to[:, s % 2], raw[:, s % 2], ACT.Copy).then_inc(hi_ready, 1)

            with act.Fori(0, DEPTH) as l:
                for t in range(TB):
                    if t == 2:
                        for s in range(2):
                            hi(l * LAYER_SLABS, s, l * LAYER_USES + 2)
                    act.wait_ge(x_ready, l * TB + t + 1)
                    if t:
                        act.wait_ge(x_sq, l * TB + t)
                    act.activation(junk[:, 0:D], xres[:, t, :], ACT.Square, accum_out=ss_x[:, t:t + 1]).then_inc(x_sq, 1)
                act.dma_start(residual.rearrange("(t p) n -> p t n", p=P), xres).then_inc(saved, 16)
                act.wait_ge(par_ld, l * 16 + 16)
                for n in range(2 * TB):
                    t, half = n // 2, n % 2
                    bank_t = (ps_t if half == 0 else ps_s)[:].rearrange("p (c n) -> p c n", c=KC // 2)
                    act.wait_ge(x_tr, l * 2 * TB + n + 1)
                    act.activation(h_hi[:, half * 4:half * 4 + 4, t * P:(t + 1) * P], bank_t, ACT.Copy)\
                        .then_inc(h_hi_ready, 1)
                with act.Fori(0, KV_HEADS) as g:
                    base = l * LAYER_SLABS + g * GROUP_SLABS
                    use = l * LAYER_USES + g * GROUP_USES + 2
                    kg = l * KV_HEADS + g
                    for t in range(TB):
                        act.wait_ge(mm_done, use + t + 1)
                        if t == TB - 1:
                            hi(base + 2, 0, use + TB + 1)
                            hi(base + 2, 1, use + TB)
                        if t:
                            act.wait_ge(k_sq, kg * TB + t)
                        act.activation(k_junk, bank[t][:, 0:P], ACT.Square, accum_out=ss_k[:, t:t + 1])\
                            .then_inc(k_sq, 1)
                        act.activation(v_hi[:, t, :], bank[t][:, P:2 * P], ACT.Copy).then_inc(v_hi_ready, 1)

                    def unit(i, first):
                        base = l * LAYER_SLABS + g * GROUP_SLABS + i * UT + 2
                        use = l * LAYER_USES + g * GROUP_USES + i * UT + TB + 2
                        turns = l * LAYER_TURNS + g * (GROUP_USES // BANKS) + i * (UT // BANKS) + 1
                        u = l * HEADS + g * GROUP + i
                        j = g * GROUP + i
                        rope = kg * (GROUP + 1) + i + 1

                        def exps(t):
                            act.wait_ge(s_nb, u * TB + t + 1)
                            act.activation(probs[:, t, :], ps_s[:], ACT.Exp, bias=nb[:, t:t + 1],
                                           scale=srq[:, t:t + 1], accum_out=rs[:, t:t + 1]).then_inc(s_exp, 1)

                        def pt_part(t):
                            act.wait_ge(pt_tr, u * TB + t + 1)
                            if t >= 2:
                                act.wait_ge(pv_done, u * TB + t - 1)
                            act.activation(pt_hi[:, t % 2, :], ps_t[:], ACT.Copy).then_inc(pt_hi_ready, 1)

                        if first:
                            act.wait_ge(k_tr, kg + 1)
                            act.activation(g_hi[:], ps_t[:], ACT.Copy, scale=par[:, PC_GK:PC_GK + 1]).then_inc(g_hi_ready, 1)
                        hi(base, 2, use)
                        if first:
                            act.wait_ge(roped, rope)
                            act.activation(k_hi[:], rope1[:], ACT.Copy).then_inc(r_hi_ready, 1)
                        act.activation(g_hi[:], bank[0][:], ACT.Copy, scale=par[:, PC_GQ:PC_GQ + 1]).then_inc(g_hi_ready, 1)
                        act.activation(val[:], bank[0][:], ACT.Square).then_inc(q_sq, 1)
                        hi(base, 3, use)
                        act.activation(ac_sb[:], bank[1][:], ACT.Copy).then_inc(taken[1], 1)
                        act.wait_ge(roped, rope + 1)
                        act.activation(r_hi[:], rope1[:], ACT.Copy).then_inc(r_hi_ready, 1)
                        hi(base, 4, use)
                        exps(0)
                        exps(1)
                        hi(base, 5, use)
                        exps(2)
                        exps(3)
                        hi(base, 6, use)
                        act.activation(gate[:], bank[0][:], ACT.Tanh, scale=0.5).then_inc(a_tanh, 1)
                        pt_part(0)
                        hi(base, 7, use)
                        pt_part(1)
                        act.wait_ge(taken[0], taken_at(turns, 4))
                        act.activation(gate[:], bank[1][:], ACT.Tanh, scale=0.5).then_inc(b_tanh, 1)
                        act.wait_ge(a_val, u + 1)
                        act.activation(p1_hi[:, j, :], val[:], ACT.Copy, scale=0.5).then_inc(a_hi, 1)
                        pt_part(2)
                        hi(base, 8, use)
                        act.wait_ge(taken[1], taken_at(turns, 5))
                        act.activation(gate[:], bank[2][:], ACT.Tanh, scale=0.5).then_inc(taken[2], 1)
                        pt_part(3)
                        hi(base, 9, use)
                        act.wait_ge(b_val, u + 1)
                        act.activation(p2_hi[:, j, :], bval[:], ACT.Copy, scale=0.5).then_inc(b_hi, 1)

                    unit(0, True)
                    with act.Fori(1, GROUP) as i:
                        unit(i, False)

                def gates(stage_slab, stage_use, squares=False):
                    with act.Fori(0, KC // 2) as jj:
                        base = l * LAYER_SLABS + stage_slab + jj * 4
                        use = l * LAYER_USES + stage_use + jj * 4 + 2
                        turns = l * LAYER_TURNS + stage_use // BANKS + jj
                        for s in range(2):
                            hi(base, 2 * s + 2, use)
                            act.wait_ge(taken[(2 * s + 3) % BANKS], taken_at(turns, 2 * s - 1))
                            act.activation(gate[:], bank[2 * s][:], ACT.Tanh, scale=0.5).then_inc(taken[2 * s], 1)
                            if squares:
                                act.wait_ge(ln_xc, l * KC + jj * 2 + s + 1)
                                act.activation(sq[:, jj * 2 + s, :], cc[:, jj * 2 + s + 1, :], ACT.Square).then_inc(ln_sq, 1)
                            hi(base, 2 * s + 3, use)

                gates(SLAB_A, USE_A)
                act.dma_start(gpost[:], post_gain[l].broadcast_to((P, D))).then_inc(post_ld, 16)
                act.dma_start(gpre[:], pre_gain[l + 1].broadcast_to((P, D))).then_inc(pre_ld, 16)
                gates(SLAB_B, USE_B, True)
                act.wait_ge(ln_var, l + 1)
                act.activation(val[:], ps_s[:], ACT.Sqrt, bias=ln_eps[:]).then_inc(ln_sd, 1)
                base = l * LAYER_SLABS + SLAB_G
                use = l * LAYER_USES + USE_G + 2
                for c in range(KC):
                    n = l * KC + c
                    act.wait_ge(n_n, n + 1)
                    if c:
                        act.wait_ge(n_s, n)
                    act.activation(ac_sb[:], cc[:, c + 1, :], ACT.Tanh, scale=0.5).then_inc(n_t, 1)
                    hi(base, c + 2, use)
                    if c:
                        act.wait_ge(taken[(c - 1) % BANKS], taken_at(l * LAYER_TURNS + USE_G // BANKS, c - 1))
                    act.activation(gate[:], bank[c % BANKS][:], ACT.Tanh, scale=0.5).then_inc(g_t, 1)
                    act.wait_ge(n_v, n + 1)
                    act.activation(p1_hi[:, c, :], bval[:], ACT.Copy, scale=0.25).then_inc(n_hi, 1)
                for t in range(TB):
                    act.dma_start(xres[:, t, :], residual[t * P:(t + 1) * P, :]).then_inc(xr_ld[t], 16)
                act.dma_start(par[:], params[l + 1]).then_inc(par_ld, 16)
                gates(SLAB_C, USE_C)
                base = l * LAYER_SLABS + SLAB_O
                use = l * LAYER_USES + USE_O + 2
                for q in range(QUARTERS):
                    if q + 1 < QUARTERS:
                        for s in range(2):
                            hi(base + 2 * q + 2, s, use + q * TB + 1 - s, alt_hi if q % 2 == 0 else w_hi)
                    for t in range(TB):
                        act.wait_ge(mm_done, use + q * TB + t + 1)
                        if q or t:
                            act.wait_ge(o_sq, (l * QUARTERS + q) * TB + t)
                        act.activation(junk[:, 0:2 * P], bank[t][:, 0:2 * P], ACT.Square,
                                       accum_out=ss_o[:, t, q:q + 1]).then_inc(o_sq, 1)
                act.wait_ge(o_sq, (l + 1) * QUARTERS * TB)
            for t in range(TB):
                act.wait_ge(x_ready, DEPTH * TB + t + 1)
                act.dma_start(out[t * P:(t + 1) * P, :], xres[:, t, :]).then_inc(store, 16)
            act.wait_ge(store, TB * 16)

        @block.tensor
        def _(pe):
            pe.wait_ge(setup, 6)
            pe.wait_ge(const_ld, 4 * 16)
            pe.wait_ge(rot_ready, 1)

            def product(out, k, hi_a, lo_a, hi_b, lo_b, first, last):
                pe.matmul(out, hi_a, hi_b, start=first, stop=False)
                pe.matmul(out, hi_a, lo_b, start=False, stop=False)
                return pe.matmul(out, lo_a, hi_b, start=False, stop=last)

            def half_tile(slab, s, turns, b, act_hi, act_lo, part, ready=None):
                out = bank[b % BANKS][:]
                if part == 0:
                    pe.wait_ge(lo_ready, slab + s + 3)
                    pe.wait_ge(taken[b % BANKS], free_at(turns, b))
                if ready:
                    pe.wait_ge(*ready)
                for k in range(part * KC // 2, (part + 1) * KC // 2):
                    mm = product(out, k, w_hi[:, s % 2, k, :], w_lo[:, s % 2, k, :], act_hi[:, k, :], act_lo[:, k, :],
                                 k == 0, k == KC - 1)
                if part == 1:
                    mm.then_inc(mm_done, 1)

            def tile(slab, s, turns, b, act_hi=h_hi, act_lo=h_lo):
                half_tile(slab, s, turns, b, act_hi, act_lo, 0)
                half_tile(slab, s, turns, b, act_hi, act_lo, 1)

            with pe.Fori(0, DEPTH) as l:
                for n in range(2 * TB):
                    t, half = n // 2, n % 2
                    to = ps_t if half == 0 else ps_s
                    if half == 0:
                        pe.wait_ge(xn_ready, l * TB + t + 1)
                    if n >= 2:
                        pe.wait_ge(h_lo_ready, l * 2 * TB + n - 1)
                    for c in range(4):
                        mm = pe.transpose(to[:, c * P:(c + 1) * P], xn[:, t % 2, (half * 4 + c) * P:(half * 4 + c + 1) * P],
                                          ident_sb[:])
                    mm.then_inc(x_tr, 1)
                with pe.Fori(0, KV_HEADS) as g:
                    pe.wait_ge(h_lo_ready, l * 2 * TB + 2 * TB)
                    kg = l * KV_HEADS + g
                    base = l * LAYER_SLABS + g * GROUP_SLABS
                    turns = l * LAYER_TURNS + g * (GROUP_USES // BANKS)
                    pe.wait_ge(lo_ready, base + 1 + 3)
                    for t in range(TB):
                        pe.wait_ge(taken[t], free_at(turns, t))
                        ts = slice(t * P, (t + 1) * P)
                        for k in range(KC):
                            mm = product(bank[t][:, 0:2 * P], k, h_hi[:, k, ts], h_lo[:, k, ts], w_hi[:, :, k, :],
                                         w_lo[:, :, k, :], k == 0, k == KC - 1)
                        mm.then_inc(mm_done, 1)
                    def rotate(n):
                        pe.wait_ge(g_lo_ready, n)
                        pe.matmul(ps_t[:], rot_r[:], g_hi[:], start=True, stop=False)
                        pe.matmul(ps_t[:], rot_r[:], g_lo[:], start=False, stop=True).then_inc(rot_done, 1)

                    def unit(i, first):
                        base = l * LAYER_SLABS + g * GROUP_SLABS + i * UT + 2
                        turns = l * LAYER_TURNS + g * (GROUP_USES // BANKS) + i * (UT // BANKS) + 1
                        u = l * HEADS + g * GROUP + i
                        rope = kg * (GROUP + 1) + i + 1

                        def part(s, n):
                            half_tile(base, s, turns, s, h_hi, h_lo, n)

                        def scores(t):
                            pe.wait_ge(r_lo_ready, rope + 1)
                            ts = slice(t * P, (t + 1) * P)
                            if t == 0:
                                pe.wait_ge(q_ms, u + 1)
                            else:
                                pe.wait_ge(s_exp, u * TB + t)
                            product(ps_s[:], 0, r_hi[:, ts], r_lo[:, ts], k_hi[:], k_lo[:], True, True).then_inc(s_done, 1)

                        def turn(b):
                            if b == 0:
                                pe.wait_ge(p_ready, u * TB + TB)
                            else:
                                pe.wait_ge(pt_lo_ready, u * TB + b)
                            for t in range(TB):
                                mm = pe.transpose(ps_t[:, t * P:(t + 1) * P], probs[:, t, b * P:(b + 1) * P], ident_sb[:])
                            mm.then_inc(pt_tr, 1)

                        def pv(b):
                            pe.wait_ge(pt_lo_ready, u * TB + b + 1)
                            product(ps_o[:], b, v_hi[:, b, :], v_lo[:, b, :], pt_hi[:, b % 2, :], pt_lo[:, b % 2, :],
                                    b == 0, b == TB - 1).then_inc(pv_done, 1)

                        part(0, 0)
                        if first:
                            pe.wait_ge(k_norm, kg + 1)
                            for t in range(TB):
                                mm = pe.transpose(ps_t[:, t * P:(t + 1) * P], k_raw[:, t, :], ident_sb[:])
                            mm.then_inc(k_tr, 1)
                        part(0, 1)
                        if first:
                            pe.wait_ge(rope1_ready, kg + 1)
                            rotate(rope)
                        part(1, 0)
                        pe.wait_ge(q_sq, u + 1)
                        for t in range(TB):
                            mm = pe.matmul(ps_s[:, t:t + 1], val[:, t * P:(t + 1) * P], ones[:], start=True, stop=True)
                        mm.then_inc(q_ss, 1)
                        part(1, 1)
                        rotate(rope + 1)
                        part(2, 0)
                        part(2, 1)
                        scores(0)
                        part(3, 0)
                        scores(1)
                        part(3, 1)
                        scores(2)
                        part(4, 0)
                        scores(3)
                        part(4, 1)
                        part(5, 0)
                        turn(0)
                        part(5, 1)
                        turn(1)
                        pv(0)
                        part(6, 0)
                        turn(2)
                        pv(1)
                        part(6, 1)
                        turn(3)
                        pv(2)
                        part(7, 0)
                        pv(3)
                        part(7, 1)

                    unit(0, True)
                    with pe.Fori(1, GROUP) as i:
                        unit(i, False)

                def projection(slab_at, use_at, ready, value, in_hi, in_lo):
                    with pe.Fori(0, KC // 2) as jj:
                        base = l * LAYER_SLABS + slab_at + jj * 4
                        turns = l * LAYER_TURNS + use_at // BANKS + jj
                        for s in range(2):
                            tile(base, 2 * s, turns, 2 * s)
                            half_tile(base, 2 * s + 1, turns, 2 * s + 1, in_hi, in_lo, 0, (ready, value - KC // 2))
                            half_tile(base, 2 * s + 1, turns, 2 * s + 1, in_hi, in_lo, 1, (ready, value))

                projection(SLAB_A, USE_A, a_lo, l * KC + KC, p1_hi, p1_lo)
                pe.wait_ge(c_ready, l * (KC + 1) + KC + 2)
                for j in range(KC):
                    mm = pe.matmul(ps_o[:], mean_w[:], cc[:, j + 1, :], start=j == 0, stop=j == KC - 1)
                mm.then_inc(ln_mean, 1)
                projection(SLAB_B, USE_B, b_lo, l * KC + KC, p2_hi, p2_lo)
                pe.wait_ge(ln_sq, l * KC + KC)
                for j in range(KC):
                    mm = pe.matmul(ps_s[:], mean_w[:], sq[:, j, :], start=j == 0, stop=j == KC - 1)
                mm.then_inc(ln_var, 1)
                with pe.Fori(0, 2) as jj:
                    for c in range(KC // 2):
                        tile(l * LAYER_SLABS + SLAB_G + jj * 4, c, l * LAYER_TURNS + USE_G // BANKS + jj, c)
                projection(SLAB_C, USE_C, n_lo, l * KC + KC, p1_hi, p1_lo)
                base = l * LAYER_SLABS + SLAB_O
                turns = l * LAYER_TURNS + USE_O // BANKS
                for q in range(QUARTERS):
                    o_hi, o_lo = (w_hi, w_lo) if q % 2 == 0 else (alt_hi, alt_lo)
                    pe.wait_ge(lo_ready, base + 2 * q + 1 + 3)
                    for t in range(TB):
                        pe.wait_ge(taken[t], free_at(turns, q * TB + t))
                        ts = slice(t * P, (t + 1) * P)
                        for k in range(KC):
                            if q == 0 and t == 0:
                                pe.wait_ge(y_lo, l * KC + k + 1)
                            mm = product(bank[t][:, 0:2 * P], k, p2_hi[:, k, ts], p2_lo[:, k, ts], o_hi[:, :, k, :],
                                         o_lo[:, :, k, :], k == 0, k == KC - 1)
                        mm.then_inc(mm_done, 1)

        @block.vector
        def _(dve):
            dve.wait_ge(setup, 6)
            dve.wait_ge(const_ld, 4 * 16)
            for t in range(TB):
                dve.wait_ge(xr_ld[t], 16)
                dve.memset(ri[:, t:t + 1], 0.0).then_inc(x_ready, 1)

            def minus(out, full, scale, hi_part, done):
                return dve.scalar_tensor_tensor(out, full, scale, hi_part.bitcast(F32), ALU.mult, ALU.subtract)\
                    .then_inc(done, 1)

            def conv_c(n, chunk, turns):
                first = n * TAPS_C
                dve.tensor_scalar(ctap[:], par[:, PC_C:PC_C + (KC + 1) * TAPS_C]
                                  .rearrange("p (c t) -> p c t", t=TAPS_C)[:, chunk, :], 0.5, None, ALU.mult)\
                    .then_inc(taps_ready, 1)
                dve.tensor_scalar(cbias[:], par[:, bass.ds(chunk + PC_BIAS, 1)], 1.0, None, ALU.mult)\
                    .then_inc(taps_ready, 1)
                for m in range(TAPS_C):
                    source = upad[:, m:m + SEQ]
                    w = ctap[:, m:m + 1]
                    if m == 0:
                        dve.wait_ge(taken[BANKS - 1], free_at(turns, 0))
                        dve.wait_ge(taps_ready, n * 2 + 2)
                        dve.wait_ge(c_ready, n + 1)
                        dve.tensor_scalar(ps_c[:], source, w, cbias[:], ALU.mult, ALU.add).then_inc(c_step, 1)
                    elif m == 1:
                        dve.tensor_scalar(acc1[:], source, w, None, ALU.mult).then_inc(c_step, 1)
                    else:
                        to = (ps_c if m % 2 == 0 else acc1)[:]
                        dve.wait_ge(c_step, first + m - 1)
                        dve.scalar_tensor_tensor(to, source, w, to, ALU.mult, ALU.add).then_inc(c_step, 1)
                    yield
                dve.wait_ge(c_step, first + TAPS_C)
                dve.tensor_tensor(cc[:, chunk, :], ps_c[:], acc1[:], ALU.add).then_inc(c_ready, 1)

            with dve.Fori(0, DEPTH) as l:
                def normed(t):
                    dve.wait_ge(x_sq, l * TB + t + 1)
                    dve.tensor_scalar(ms_x[:, t:t + 1], ss_x[:, t:t + 1], 1.0 / D, RMS_EPS, ALU.mult, ALU.add).then_inc(x_ms, 1)
                    if t == 0:
                        dve.wait_ge(pre_ld, l * 16 + 16)
                    dve.wait_ge(x_r, l * TB + t + 1)
                    if t >= 2:
                        dve.wait_ge(x_tr, l * 2 * TB + 2 * (t - 1))
                    dve.scalar_tensor_tensor(xn[:, t % 2, :], xres[:, t, :], rx[:, t:t + 1], gpre[:], ALU.mult, ALU.mult)\
                        .then_inc(xn_ready, 1)

                normed(0)
                normed(1)
                for n in range(2 * TB):
                    t, half = n // 2, n % 2
                    bank_t = (ps_t if half == 0 else ps_s)[:].rearrange("p (c n) -> p c n", c=KC // 2)
                    dve.wait_ge(h_hi_ready, l * 2 * TB + n + 1)
                    dve.tensor_tensor(h_lo[:, half * 4:half * 4 + 4, t * P:(t + 1) * P], bank_t,
                                      h_hi[:, half * 4:half * 4 + 4, t * P:(t + 1) * P].bitcast(F32), ALU.subtract)\
                        .then_inc(h_lo_ready, 1)
                    if half == 1 and t + 2 < TB:
                        normed(t + 2)
                with dve.Fori(0, KV_HEADS) as g:
                    dve.wait_ge(saved, l * 16 + 16)
                    kg = l * KV_HEADS + g
                    for t in range(TB):
                        dve.wait_ge(v_hi_ready, kg * TB + t + 1)
                        dve.wait_ge(k_sq, kg * TB + t + 1)
                        dve.tensor_copy(k_raw[:, t, :], bank[t][:, 0:P]).then_inc(k_copied, 1)
                        dve.tensor_tensor(v_lo[:, t, :], bank[t][:, P:2 * P], v_hi[:, t, :].bitcast(F32), ALU.subtract)\
                            .then_inc(taken[t], 1)
                    dve.tensor_scalar(ms_k[:], ss_k[:], 1.0 / P, RMS_EPS, ALU.mult, ALU.add).then_inc(k_ms, 1)
                    dve.wait_ge(k_r, kg + 1)
                    dve.wait_ge(k_copied, kg * TB + TB)
                    for t in range(TB):
                        k_scaled = dve.tensor_scalar(k_raw[:, t, :], k_raw[:, t, :], rk[:, t:t + 1], None, ALU.mult)
                    k_scaled.then_inc(k_norm, 1)

                    def rope(source, gain, n, squared, done):
                        dve.wait_ge(g_hi_ready, n)
                        if squared is not None:
                            dve.wait_ge(q_sq, squared)
                            dve.wait_ge(r_lo_ready, n - 1)
                        minus(g_lo[:], source, gain, g_hi[:], g_lo_ready)
                        dve.scalar_tensor_tensor(rope1[:], source, gain, cos_sb[:], ALU.mult, ALU.mult).then_inc(done, 1)

                    def rope_end(n, one, value, lo_to, hi_to):
                        dve.wait_ge(rot_done, n)
                        dve.tensor_tensor(rope2[:], ps_t[:], sin_sb[:], ALU.mult).then_inc(rope2_ready, 1)
                        dve.wait_ge(rope2_ready, n)
                        dve.wait_ge(one, value)
                        dve.tensor_tensor(rope1[:], rope1[:], rope2[:], ALU.add).then_inc(roped, 1)
                        dve.wait_ge(r_hi_ready, n)
                        dve.wait_ge(roped, n)
                        dve.tensor_tensor(lo_to[:], rope1[:], hi_to[:].bitcast(F32), ALU.subtract).then_inc(r_lo_ready, 1)

                    def unit(i, first):
                        use = l * LAYER_USES + g * GROUP_USES + i * UT + TB + 2
                        turns = l * LAYER_TURNS + g * (GROUP_USES // BANKS) + i * (UT // BANKS) + 1
                        u = l * HEADS + g * GROUP + i
                        j = g * GROUP + i
                        n_rope = kg * (GROUP + 1) + i + 2
                        conv = conv_c(l * (KC + 1) + j, j, turns)

                        def taps(n):
                            for _ in range(n):
                                next(conv, None)

                        def softmax_max(t):
                            dve.wait_ge(s_done, u * TB + t + 1)
                            dve.tensor_reduce(mx[:, t:t + 1], ps_s[:], AX_X, ALU.max).then_inc(s_max, 1)
                            if t == 0:
                                dve.wait_ge(q_r, u + 1)
                                dve.tensor_scalar(srq[:], rq[:], SCALE, None, ALU.mult).then_inc(q_sr, 1)
                                dve.wait_ge(q_sr, u + 1)
                            dve.wait_ge(s_max, u * TB + t + 1)
                            dve.tensor_scalar(nb[:, t:t + 1], mx[:, t:t + 1], srq[:, t:t + 1], -1.0, ALU.mult, ALU.mult)\
                                .then_inc(s_nb, 1)

                        def softmax_end(t):
                            dve.wait_ge(s_exp, u * TB + t + 1)
                            dve.reciprocal(ri[:, t:t + 1], rs[:, t:t + 1]).then_inc(s_ri, 1)
                            dve.wait_ge(s_ri, u * TB + t + 1)
                            dve.tensor_scalar(probs[:, t, :], probs[:, t, :], ri[:, t:t + 1], None, ALU.mult).then_inc(p_ready, 1)

                        def pt_rest(t):
                            dve.wait_ge(pt_hi_ready, u * TB + t + 1)
                            dve.tensor_tensor(pt_lo[:, t % 2, :], ps_t[:], pt_hi[:, t % 2, :].bitcast(F32), ALU.subtract)\
                                .then_inc(pt_lo_ready, 1)

                        if first:
                            dve.wait_ge(k_tr, kg + 1)
                            rope(ps_t[:], par[:, PC_GK:PC_GK + 1], n_rope - 1, None, rope1_ready)
                        taps(2)
                        if first:
                            rope_end(n_rope - 1, rope1_ready, kg + 1, k_lo, k_hi)
                        rope(bank[0][:], par[:, PC_GQ:PC_GQ + 1], n_rope, u + 1, taken[0])
                        taps(2)
                        dve.wait_ge(q_ss, u + 1)
                        dve.tensor_scalar(ms_q[:], ps_s[:, 0:TB], 1.0 / P, RMS_EPS, ALU.mult, ALU.add).then_inc(q_ms, 1)
                        taps(2)
                        rope_end(n_rope, taken[0], taken_at(turns, 0), r_lo, r_hi)
                        dve.tensor_scalar(atap[:], par[:, PC_A:PC_A + KC * TAPS_A]
                                          .rearrange("p (c t) -> p c t", t=TAPS_A)[:, j, :], 1.0, None, ALU.mult)\
                            .then_inc(a_conv, 1)
                        taps(3)
                        softmax_max(0)
                        dve.wait_ge(mm_done, use + 3)
                        dve.wait_ge(taken[1], taken_at(turns, 1))
                        dve.tensor_tensor(axpad[:, PAD_A:PAD_A + SEQ], bank[2][:], ac_sb[:], ALU.mult)\
                            .then_inc(taken[2], 1)
                        taps(2)
                        softmax_max(1)
                        softmax_end(0)
                        taps(1)
                        dve.wait_ge(taken[2], taken_at(turns, 2))
                        dve.wait_ge(a_conv, u * 4 + 1)
                        dve.tensor_scalar(ca[:, 0, :], axpad[:, 0:SEQ], atap[:, 0:1], None, ALU.mult).then_inc(a_conv, 1)
                        taps(1)
                        softmax_max(2)
                        softmax_end(1)
                        for m in (1, 2):
                            dve.wait_ge(a_conv, u * 4 + m + 1)
                            dve.scalar_tensor_tensor(ca[:, 0, :], axpad[:, m:m + SEQ], atap[:, m:m + 1], ca[:, 0, :],
                                                     ALU.mult, ALU.add).then_inc(a_conv, 1)
                            taps(1)
                        softmax_max(3)
                        softmax_end(2)
                        dve.wait_ge(mm_done, use + 4)
                        dve.wait_ge(a_conv, u * 4 + 4)
                        dve.tensor_tensor(ca[:, 0, :], ca[:, 0, :], bank[3][:], ALU.mult)\
                            .then_inc(taken[3], 1)
                        taps(1)
                        softmax_end(3)
                        taps(3)
                        pt_rest(0)
                        dve.wait_ge(a_tanh, u + 1)
                        dve.scalar_tensor_tensor(ca[:, 1, :], gate[:], 1.0, bank[0][:], ALU.add, ALU.mult)\
                            .then_inc(taken[0], 1)
                        taps(1)
                        pt_rest(1)
                        dve.wait_ge(taken[0], taken_at(turns, 4))
                        dve.wait_ge(taken[3], taken_at(turns, 3))
                        dve.tensor_tensor(val[:], ca[:, 0, :], ca[:, 1, :], ALU.mult).then_inc(a_val, 1)
                        taps(3)
                        pt_rest(2)
                        dve.wait_ge(a_hi, u + 1)
                        minus(p1_lo[:, j, :], val[:], 0.5, p1_hi[:, j, :], a_lo)
                        dve.wait_ge(b_tanh, u + 1)
                        dve.scalar_tensor_tensor(ca[:, 1, :], gate[:], 1.0, bank[1][:], ALU.add, ALU.mult)\
                            .then_inc(taken[1], 1)
                        taps(3)
                        pt_rest(3)
                        taps(TAPS_C)
                        dve.wait_ge(pv_done, u * TB + TB)
                        dve.wait_ge(taken[1], taken_at(turns, 5))
                        dve.tensor_tensor(bval[:], ps_o[:], ca[:, 1, :], ALU.mult).then_inc(b_val, 1)
                        dve.wait_ge(b_hi, u + 1)
                        minus(p2_lo[:, j, :], bval[:], 0.5, p2_hi[:, j, :], b_lo)
                        dve.wait_ge(taken[2], taken_at(turns, 6))
                        dve.wait_ge(mm_done, use + 8)
                        dve.scalar_tensor_tensor(upad[:, PAD_C:PAD_C + SEQ], gate[:], 1.0, bank[3][:], ALU.add, ALU.mult)\
                            .then_inc(taken[3], 1)

                    unit(0, True)
                    with dve.Fori(1, GROUP) as i:
                        unit(i, False)
                for _ in conv_c(l * (KC + 1) + KC, KC, l * LAYER_TURNS + USE_A // BANKS):
                    pass

                def merged(use_at, n):
                    with dve.Fori(0, KC // 2) as jj:
                        use = l * LAYER_USES + use_at + jj * 4 + 2
                        turns = l * LAYER_TURNS + use_at // BANKS + jj
                        for s in range(2):
                            j = jj * 2 + s
                            if n == 1:
                                dve.wait_ge(ln_mean, l + 1)
                                dve.tensor_tensor(cc[:, j + 1, :], cc[:, j + 1, :], ps_o[:], ALU.subtract).then_inc(ln_xc, 1)
                            dve.wait_ge(taken[2 * s], taken_at(turns, 2 * s))
                            dve.wait_ge(mm_done, use + 2 * s + 2)
                            to = y[:, j, :] if n == 0 else bval[:]
                            dve.scalar_tensor_tensor(to, gate[:], 1.0, bank[2 * s + 1][:], ALU.add, ALU.mult)\
                                .then_inc(taken[2 * s + 1], 1)
                            if n:
                                dve.wait_ge(taken[2 * s + 1], taken_at(turns, 2 * s + 1))
                                dve.tensor_tensor(y[:, j, :], y[:, j, :], bval[:], ALU.add).then_inc(y_ready, 1)
                                dve.wait_ge(y_ready, l * 2 * KC + (n - 1) * KC + jj * 2 + s + 1)
                            if n == 2:
                                dve.tensor_scalar(p2_hi[:, j, :], y[:, j, :], 0.5, None, ALU.mult).then_inc(y_hi, 1)
                                dve.wait_ge(y_hi, l * KC + jj * 2 + s + 1)
                                minus(p2_lo[:, j, :], y[:, j, :], 0.5, p2_hi[:, j, :], y_lo)

                merged(USE_A, 0)
                merged(USE_B, 1)
                dve.wait_ge(ln_sd, l + 1)
                dve.reciprocal(acc1[:], val[:]).then_inc(ln_r, 1)
                dve.wait_ge(ln_r, l + 1)
                dve.wait_ge(ln_xc, l * KC + KC)

                def layer_normed(c):
                    n = l * KC + c
                    dve.tensor_tensor(cc[:, c + 1, :], cc[:, c + 1, :], acc1[:], ALU.mult).then_inc(n_z, 1)
                    dve.wait_ge(n_z, n + 1)
                    dve.tensor_scalar(cc[:, c + 1, :], cc[:, c + 1, :], par[:, PC_LNG + c:PC_LNG + c + 1],
                                      par[:, PC_LNB + c:PC_LNB + c + 1], ALU.mult, ALU.add).then_inc(n_n, 1)

                layer_normed(0)
                for c in range(KC):
                    n = l * KC + c
                    dve.wait_ge(n_n, n + 1)
                    dve.wait_ge(n_t, n + 1)
                    dve.scalar_tensor_tensor(ca[:, 0, :], ac_sb[:], 1.0, cc[:, c + 1, :], ALU.add, ALU.mult).then_inc(n_s, 1)
                    if c + 1 < KC:
                        layer_normed(c + 1)
                    dve.wait_ge(g_t, n + 1)
                    dve.scalar_tensor_tensor(val[:], gate[:], 1.0, bank[c % BANKS][:], ALU.add, ALU.mult)\
                        .then_inc(taken[c % BANKS], 1)
                    dve.wait_ge(n_s, n + 1)
                    dve.wait_ge(taken[c % BANKS], taken_at(l * LAYER_TURNS + USE_G // BANKS, c))
                    dve.tensor_tensor(bval[:], val[:], ca[:, 0, :], ALU.mult).then_inc(n_v, 1)
                    dve.wait_ge(n_hi, n + 1)
                    dve.wait_ge(n_v, n + 1)
                    minus(p1_lo[:, c, :], bval[:], 0.25, p1_hi[:, c, :], n_lo)
                merged(USE_C, 2)
                for q in range(QUARTERS):
                    for t in range(TB):
                        dve.wait_ge(o_sq, (l * QUARTERS + q) * TB + t + 1)
                        dve.tensor_copy(yo[:, t, q * 2 * P:(q + 1) * 2 * P], bank[t][:, 0:2 * P])\
                            .then_inc(taken[t], 1)
                        if q == QUARTERS - 1:
                            n = l * TB + t + 1
                            dve.tensor_reduce(so[:, t:t + 1], ss_o[:, t, :], AX_X, ALU.add).then_inc(o_ss, 1)
                            dve.wait_ge(o_ss, n)
                            dve.tensor_scalar(ms_o[:, t:t + 1], so[:, t:t + 1], 1.0 / D, RMS_EPS, ALU.mult, ALU.add).then_inc(o_ms, 1)
                            if t == 0:
                                dve.wait_ge(post_ld, l * 16 + 16)
                            dve.wait_ge(xr_ld[t], l * 16 + 32)
                            dve.wait_ge(o_r, n)
                            dve.wait_ge(taken[t], taken_at(l * LAYER_TURNS + USE_O // BANKS, q * TB + t))
                            dve.scalar_tensor_tensor(yo[:, t, :], yo[:, t, :], ro[:, t:t + 1], gpost[:], ALU.mult, ALU.mult)\
                                .then_inc(o_scaled, 1)
                            dve.wait_ge(o_scaled, n)
                            dve.tensor_tensor(xres[:, t, :], xres[:, t, :], yo[:, t, :], ALU.add).then_inc(x_ready, 1)


def rope_tables():
    n_freq = P // 4
    inv_freq = (np.float32(THETA) ** (-np.arange(n_freq, dtype=np.float32) / np.float32(n_freq))).astype(np.float32)
    tokens = np.arange(SEQ)
    pos = np.stack([tokens // GRID_W, tokens % GRID_W]).astype(np.float32)
    angle = (inv_freq[None, :, None] * pos[:, None, :]).astype(np.float32)
    angle = np.repeat(angle[:, None], 2, axis=1).reshape(P, SEQ)
    return np.cos(angle).astype(np.float32), np.sin(angle).astype(np.float32)


def rotation():
    quarter = P // 4
    r = np.zeros((P, P), np.float32)
    for m in range(P):
        if m // quarter % 2 == 0:
            r[m + quarter, m] = -1.0
        else:
            r[m - quarter, m] = 1.0
    return r


def kernel(**inputs):
    import concourse.bacc as bacc
    from concourse.bass_utils import run_bass_kernel_spmd

    a = {k: np.asarray(v) for k, v in inputs.items()}
    f32 = np.float32

    blocks = {n: a[n].reshape(DEPTH, KC, P, -1, P) for n in ("w_in", "w_out_a", "w_out_b", "w_out_c", "w_o")}
    order = slab_order()
    slabs = np.empty((DEPTH * LAYER_SLABS // 2, 2, P, KC, P), f32)
    flat = slabs.reshape(DEPTH, LAYER_SLABS, P, KC, P)
    for n, (name, b) in enumerate(order):
        flat[:, n] = blocks[name][:, :, :, b, :].transpose(0, 2, 1, 3)

    params = np.zeros((DEPTH + 1, P, PC_N), f32)
    by_chunk = lambda v: v.reshape(DEPTH, -1, KC, P).transpose(0, 3, 2, 1)
    params[:DEPTH, :, PC_C + TAPS_C:PC_BIAS] = by_chunk(a["conv_c_w"]).reshape(DEPTH, P, -1)
    params[:DEPTH, :, PC_BIAS + 1:PC_A] = by_chunk(a["conv_c_b"])[..., 0]
    params[:DEPTH, :, PC_A:PC_LNG] = by_chunk(a["conv_a_w"]).reshape(DEPTH, P, -1)
    params[:DEPTH, :, PC_LNG:PC_LNB] = by_chunk(a["ln_c_g"])[..., 0]
    params[:DEPTH, :, PC_LNB:PC_GQ] = by_chunk(a["ln_c_b"])[..., 0]
    params[:DEPTH, :, PC_GQ] = a["q_norm"]
    params[:DEPTH, :, PC_GK] = a["k_norm"]
    pre = np.concatenate([a["norm_pre"], np.zeros((1, D), f32)])
    cos, sin = rope_tables()
    arrays = {
        "x": a["x"].reshape(SEQ, D), "slabs": slabs, "params": params, "pre_gain": pre.reshape(DEPTH + 1, 1, D),
        "post_gain": a["norm_post"].reshape(DEPTH, 1, D), "ident": np.eye(P, dtype=f32), "rot": rotation(), "cos": cos, "sin": sin,
    }
    nc = bacc.Bacc("TRN2", target_bir_lowering=False, num_devices=1)
    args = [nc.dram_tensor(n, v.shape, F32, kind="ExternalInput").ap() for n, v in arrays.items()]
    residual = nc.dram_tensor("residual", (SEQ, D), F32).ap()
    out = nc.dram_tensor("out", (SEQ, D), F32, kind="ExternalOutput").ap()
    encoder_kernel(nc, *args, residual, out)
    r = run_bass_kernel_spmd(nc, [arrays], core_ids=[0])
    return np.asarray(r.results[0]["out"]).reshape(1, SEQ, D)
```

```python
from contextlib import ExitStack

import numpy as np

import concourse.bass as bass
from concourse import mybir
from concourse.alu_op_type import AluOpType as ALU

F32 = mybir.dt.float32
F32R = mybir.dt.float32r
ACT = mybir.ActivationFunctionType
AX_X = mybir.AxisListType.X

P = 128
D = 1024
SEQ = 512
DEPTH = 2
KC = D // P
TB = SEQ // P
HEADS = KC
KV_HEADS = 2
GROUP = HEADS // KV_HEADS
TAPS_A, TAPS_C = 3, 31
PAD_A, PAD_C = TAPS_A // 2, TAPS_C // 2
RMS_EPS, LN_EPS = 1e-6, 1e-5
SCALE = float(P) ** -0.5
GRID_W, THETA = 64, 10000.0

SPLIT_NAMES = ("a_b", "a_c", "a_x", "a_g", "q", "k", "v", "b_g", "c_u", "c_v", "c_g", "m_a", "m_b", "m_c")
SPLIT_BLOCKS = (KC, KC, KC, KC, HEADS, KV_HEADS, KV_HEADS, KC, KC, KC, KC, KC, KC, KC)
FIRST_BLOCK = {n: sum(SPLIT_BLOCKS[:i]) for i, n in enumerate(SPLIT_NAMES)}
UNIT_TILES = ("q", "a_c", "a_x", "a_b", "a_g", "b_g", "c_v", "c_u")
UT = len(UNIT_TILES)

GROUP_SLABS = 2 + GROUP * UT
GROUP_USES = TB + GROUP * UT
SLAB_A = KV_HEADS * GROUP_SLABS
USE_A = KV_HEADS * GROUP_USES
SLAB_B, USE_B = SLAB_A + 2 * KC, USE_A + 2 * KC
SLAB_G, USE_G = SLAB_B + 2 * KC, USE_B + 2 * KC
SLAB_C, USE_C = SLAB_G + KC, USE_G + KC
SLAB_O, USE_O = SLAB_C + 2 * KC, USE_C + 2 * KC
HALVES = 2
LAYER_SLABS = SLAB_O + KC
O_ORDER = ((0, 0), (1, 0), (0, 1), (1, 1), (2, 0), (2, 1), (3, 0), (3, 1))
LAYER_USES = USE_O + len(O_ORDER)
BANKS = 4
LAYER_TURNS = LAYER_USES // BANKS

PC_C = 0
PC_BIAS = PC_C + (KC + 1) * TAPS_C
PC_A = PC_BIAS + KC + 1
PC_LNG = PC_A + KC * TAPS_A
PC_LNB = PC_LNG + KC
PC_GQ = PC_LNB + KC
PC_GK = PC_GQ + 1
PC_N = PC_GK + 1


def slab_order():
    order = []
    for g in range(KV_HEADS):
        order += [("w_in", FIRST_BLOCK["k"] + g), ("w_in", FIRST_BLOCK["v"] + g)]
        for i in range(GROUP):
            order += [("w_in", FIRST_BLOCK[n] + g * GROUP + i) for n in UNIT_TILES]
    for gate, out in (("m_a", "w_out_a"), ("m_b", "w_out_b")):
        for j in range(KC):
            order += [("w_in", FIRST_BLOCK[gate] + j), (out, j)]
    order += [("w_in", FIRST_BLOCK["c_g"] + j) for j in range(KC)]
    for j in range(KC):
        order += [("w_in", FIRST_BLOCK["m_c"] + j), ("w_out_c", j)]
    order += [("w_o", j) for j in range(KC)]
    assert len(order) == LAYER_SLABS
    return order


def encoder_kernel(nc, x, slabs, params, pre_gain, post_gain, ident, rot, cos, sin, residual, out):
    with ExitStack() as ctx:
        def sb(name, shape, dt=F32, where=ctx):
            return where.enter_context(nc.sbuf_tensor(name, shape, dt))

        def sem(name):
            return ctx.enter_context(nc.semaphore(name))

        h_hi, h_lo = sb("h_hi", [P, KC, SEQ], F32R), sb("h_lo", [P, KC, SEQ], F32R)
        with ExitStack() as p1_time:
            p1_hi, p1_lo = (sb(n, [P, KC, SEQ], F32R, p1_time) for n in ("p1_hi", "p1_lo"))
        alt_hi, alt_lo = sb("alt_hi", [P, 4, KC, P], F32R), sb("alt_lo", [P, 4, KC, P], F32R)
        p2_hi, p2_lo = sb("p2_hi", [P, KC, SEQ], F32R), sb("p2_lo", [P, KC, SEQ], F32R)
        cc = sb("cc", [P, KC + 1, SEQ])
        c_sum = cc[:, 0, :]
        xres = cc[:, 1:KC + 1, :].rearrange("p (t a) n -> p t (a n)", t=TB)
        raw = sb("raw", [P, 2, KC, P])
        w_hi, w_lo = sb("w_hi", [P, 2, KC, P], F32R), sb("w_lo", [P, 2, KC, P], F32R)
        with ExitStack() as attention_time:
            k_hi, k_lo = (sb(n, [P, SEQ], F32R, attention_time) for n in ("k_hi", "k_lo"))
            v_hi, v_lo = (sb(n, [P, TB, P], F32R, attention_time) for n in ("v_hi", "v_lo"))
            probs = sb("probs", [P, TB, SEQ], F32, attention_time)
            pt_hi, pt_lo = (sb(n, [P, 2, SEQ], F32R, attention_time) for n in ("pt_hi", "pt_lo"))
            with ExitStack() as rotation_time:
                g_hi, g_lo = (sb(n, [P, SEQ], F32R, rotation_time) for n in ("g_hi", "g_lo"))
                r_hi, r_lo = (sb(n, [P, SEQ], F32R, rotation_time) for n in ("r_hi", "r_lo"))
            last_hi, last_lo = (sb(n, [P, KC, P], F32R, attention_time) for n in ("last_hi", "last_lo"))
            rope1, rope2 = (sb(n, [P, SEQ], F32, attention_time) for n in ("rope1", "rope2"))
        k_raw = probs[:, 0, :].rearrange("p (t n) -> p t n", t=TB)
        k_junk = probs[:, 1, 0:P]
        first_hi, first_lo = (a[:].rearrange("p a (b n) -> p (a b) n", n=P) for a in (pt_hi, pt_lo))
        with ExitStack() as y_time:
            y = sb("y", [P, KC, SEQ], F32, y_time)
            sq = sb("sq", [P, 2, SEQ], F32, y_time)
            o_hi, o_lo = (sb(n, [P, 2, KC, P], F32R, y_time) for n in ("o_hi", "o_lo"))
        xn0 = sb("xn0", [P, D])
        yo = sb("yo", [P, 2, D])
        xn1 = sb("xn1", [P, D])
        xn = (xn0, xn1)
        junk = sb("junk", [P, D])
        sb("attention_rest", [P, 4 * D])
        gpost = sb("gpost", [P, D])
        rot_f = gpost[:, 0:P]
        cos_sb, sin_sb = sb("cos_sb", [P, SEQ]), sb("sin_sb", [P, SEQ])
        upad = sb("upad", [P, SEQ + 2 * PAD_C])
        axpad = sb("axpad", [P, SEQ + 2 * PAD_A])
        gpre = sb("gpre", [P, D])
        acc1 = sb("acc1", [P, SEQ])
        gate = sb("gate", [P, SEQ])
        ac_sb = sb("ac_sb", [P, SEQ])
        ca = sb("ca", [P, 2, SEQ])
        val = sb("val", [P, SEQ])
        bval = sb("bval", [P, SEQ])
        par = sb("par", [P, PC_N])
        ctap, atap, cbias = sb("ctap", [P, TAPS_C]), sb("atap", [P, TAPS_A]), sb("cbias", [P, 1])
        ident_sb, rot_r = sb("ident_sb", [P, P]), sb("rot_r", [P, P], F32R)
        mean_w = sb("mean_w", [P, P])
        ones = sb("ones", [P, 1])
        ln_eps = sb("ln_eps", [P, 1])
        half_neg = sb("half_neg", [P, TB])
        ss_x, ms_x, rx = (sb(n, [P, TB]) for n in ("ss_x", "ms_x", "rx"))
        ss_k, ms_k, rk = (sb(n, [P, TB]) for n in ("ss_k", "ms_k", "rk"))
        ms_q, rq, srq = (sb(n, [P, TB]) for n in ("ms_q", "rq", "srq"))
        ss_o = sb("ss_o", [P, TB, HALVES])
        half_ms, ms_o, ro = (sb(n, [P, TB]) for n in ("half_ms", "ms_o", "ro"))
        mx, nb, rs, ri = (sb(n, [P, TB]) for n in ("mx", "nb", "rs", "ri"))

        bank = [ctx.enter_context(nc.psum_tensor(f"bank{i}", [P, SEQ], F32)) for i in range(BANKS)]
        ps_s, ps_t, ps_o, ps_c = (ctx.enter_context(nc.psum_tensor(n, [P, SEQ], F32)) for n in ("ps_s", "ps_t", "ps_o", "ps_c"))

        const_ld, ident_ld, rot_ld, saved, store = sem("const_ld"), sem("ident_ld"), sem("rot_ld"), sem("saved"), sem("store")
        xr_ld = [sem(f"xr_ld{t}") for t in range(TB)]
        pre_ld, post_ld = sem("pre_ld"), sem("post_ld")
        slab_ld = [sem(f"slab_ld{i}") for i in range(2)]
        hi_ready, lo_ready = sem("hi_ready"), sem("lo_ready")
        mm_done = sem("mm_done")
        taken = [sem(f"taken{i}") for i in range(BANKS)]
        setup = sem("setup")
        rot_ready, par_ld, taps_ready = sem("rot_ready"), sem("par_ld"), sem("taps_ready")
        x_ready, x_sq, x_ms, x_r, xn_ready, x_tr, h_hi_ready, h_lo_ready = (
            sem(n) for n in ("x_ready", "x_sq", "x_ms", "x_r", "xn_ready", "x_tr", "h_hi_ready", "h_lo_ready"))
        k_sq, k_copied, v_hi_ready, k_ms, k_r, k_norm, k_tr = (
            sem(n) for n in ("k_sq", "k_copied", "v_hi_ready", "k_ms", "k_r", "k_norm", "k_tr"))
        g_hi_ready, g_lo_ready, rope1_ready, rot_done, rope2_ready, roped, r_hi_ready, r_lo_ready = (
            sem(n) for n in ("g_hi_ready", "g_lo_ready", "rope1_ready", "rot_done", "rope2_ready", "roped", "r_hi_ready", "r_lo_ready"))
        q_sq, q_ss, q_ms, q_r, q_sr = (sem(n) for n in ("q_sq", "q_ss", "q_ms", "q_r", "q_sr"))
        s_done, s_max, s_nb, s_exp, s_ri, p_ready = (sem(n) for n in ("s_done", "s_max", "s_nb", "s_exp", "s_ri", "p_ready"))
        pt_tr, pt_hi_ready, pt_lo_ready, pv_done = (sem(n) for n in ("pt_tr", "pt_hi_ready", "pt_lo_ready", "pv_done"))
        b_tanh, b_val, b_hi, b_lo = (sem(n) for n in ("b_tanh", "b_val", "b_hi", "b_lo"))
        a_conv, a_tanh, a_val, a_hi, a_lo = (
            sem(n) for n in ("a_conv", "a_tanh", "a_val", "a_hi", "a_lo"))
        c_step, c_ready, c_summed = sem("c_step"), sem("c_ready"), sem("c_summed")
        m_tanh, m_val, y_ready, y_hi, y_lo = (sem(n) for n in ("m_tanh", "m_val", "y_ready", "y_hi", "y_lo"))
        ln_mean, ln_xc, ln_sq, ln_sum, ln_var, ln_sd, ln_r = (
            sem(n) for n in ("ln_mean", "ln_xc", "ln_sq", "ln_sum", "ln_var", "ln_sd", "ln_r"))
        n_z, n_n, n_t, n_s, g_t, n_v, n_hi, n_lo = (
            sem(n) for n in ("n_z", "n_n", "n_t", "n_s", "g_t", "n_v", "n_hi", "n_lo"))
        o_sq, o_half, o_ms, o_r, o_scaled = (sem(n) for n in ("o_sq", "o_half", "o_ms", "o_r", "o_scaled"))

        def free_at(turns, b):
            return turns + b // BANKS + 1

        def taken_at(turns, b):
            return turns + b // BANKS + 2

        block = ctx.enter_context(nc.Block())

        @block.sync
        def _(sp):
            with sp.Fori(0, DEPTH * LAYER_SLABS // 2 + 1) as n2:
                for s in range(2):
                    sp.wait_ge(lo_ready, n2 * 2 + s + 1)
                    sp.dma_start(raw[:, s, :, :], slabs[n2, s]).then_inc(slab_ld[s], 16)
            for t in range(TB):
                sp.wait_ge(x_ready, DEPTH * TB + t + 1)
                sp.dma_start(out[t * P:(t + 1) * P, :], xres[:, t, :]).then_inc(store, 16)
            sp.wait_ge(store, TB * 16)
            sp.wait_ge(par_ld, (DEPTH + 1) * 16)
            sp.wait_ge(pre_ld, (DEPTH + 1) * 16)

        @block.gpsimd
        def _(pool):
            pool.memset(ones[:], 1.0).then_inc(setup, 1)
            pool.memset(mean_w[:], 1.0 / D).then_inc(setup, 1)
            pool.memset(half_neg[:], -0.5).then_inc(setup, 1)
            pool.memset(ln_eps[:], LN_EPS).then_inc(setup, 1)
            pool.memset(upad[:], 0.0).then_inc(setup, 1)
            pool.memset(axpad[:], 0.0).then_inc(setup, 1)
            pool.memset(rs[:, 0:1], 0.0).then_inc(lo_ready, 2)
            pool.memset(rs[:, 1:2], 0.0).then_inc(mm_done, 2)
            pool.memset(rs[:, 2:3], 0.0).then_inc(c_ready, 1)
            for b in range(BANKS):
                pool.memset(mx[:, b:b + 1], 0.0).then_inc(taken[b], 1)
            pool.wait_ge(setup, 6)
            pool.wait_ge(rot_ld, 16)
            pool.tensor_copy(rot_r[:], rot_f).then_inc(rot_ready, 1)

            def lo(base, s, hi_part=None, to=None):
                if to is None:
                    hi_part, to = w_hi[:, s % 2], w_lo[:, s % 2]
                pool.wait_ge(hi_ready, base + s + 1)
                pool.tensor_tensor(to, raw[:, s % 2], hi_part.bitcast(F32), ALU.subtract)\
                    .then_inc(lo_ready, 1)

            def power(ready, value, out, ms, done):
                pool.wait_ge(ready, value)
                pool.tensor_tensor(out, ms, half_neg[:, 0:out.shape[1]], ALU.pow).then_inc(done, 1)

            def x_power(n, t):
                power(x_ms, n * TB + t + 1, rx[:, t:t + 1], ms_x[:, t:t + 1], x_r)

            def first_slabs(base):
                lo(base, 0)
                lo(base, 1)

            for t in range(3):
                x_power(0, t)
            first_slabs(0)
            with pool.Fori(0, DEPTH) as l:
                x_power(l, 3)

                def group(g):
                    lo(l * LAYER_SLABS + g * GROUP_SLABS + 2, 0, first_hi, first_lo)
                    lo(l * LAYER_SLABS + g * GROUP_SLABS + 2, 1)
                    power(k_ms, l * KV_HEADS + g + 1, rk[:], ms_k[:], k_r)
                    with pool.Fori(0, GROUP) as i:
                        base = l * LAYER_SLABS + g * GROUP_SLABS + i * UT + 2
                        u = l * HEADS + g * GROUP + i
                        for s in range(2, UT + 2):
                            own = (last_hi[:], last_lo[:]) if s == UT - 1 else ()
                            lo(base, s, *own)
                            if s == 2:
                                power(q_ms, u + 1, rq[:], ms_q[:], q_r)
                group(0)
                with pool.Fori(1, KV_HEADS) as g:
                    group(g)
                with pool.Fori(0, (SLAB_O - SLAB_A) // 2 - 1) as j:
                    for s in range(2):
                        lo(l * LAYER_SLABS + SLAB_A + 2 + j * 2, s)
                o_base = l * LAYER_SLABS + SLAB_O
                for s in range(KC):
                    if s // 2 == 0:
                        lo(o_base, s, o_hi[:, s], o_lo[:, s])
                    elif s // 2 == 1:
                        lo(o_base, s)
                    else:
                        lo(o_base, s, alt_hi[:, s - 4], alt_lo[:, s - 4])

                def o_power(t):
                    power(o_ms, l * TB + t + 1, ro[:, t:t + 1], ms_o[:, t:t + 1], o_r)

                o_power(0)
                o_power(1)
                x_power(l + 1, 0)
                x_power(l + 1, 1)
                o_power(2)
                x_power(l + 1, 2)
                first_slabs((l + 1) * LAYER_SLABS)
                o_power(3)

        @block.scalar
        def _(act):
            for t in range(TB):
                act.dma_start(xres[:, t, :], x[t * P:(t + 1) * P, :]).then_inc(xr_ld[t], 16)
                if t == 0:
                    act.dma_start(rot_f, rot).then_inc(rot_ld, 16)
                    act.dma_start(gpre[:], pre_gain[0].broadcast_to((P, D))).then_inc(pre_ld, 16)
                    act.dma_start(ident_sb[:], ident).then_inc(ident_ld, 16)
            act.dma_start(cos_sb[:], cos).then_inc(const_ld, 16)
            act.dma_start(sin_sb[:], sin).then_inc(const_ld, 16)
            act.dma_start(par[:], params[0]).then_inc(par_ld, 16)

            def split(base, s, to=None):
                act.wait_ge(slab_ld[s % 2], base * 8 + (s // 2 + 1) * 16)
                act.activation(w_hi[:, s % 2] if to is None else to, raw[:, s % 2], ACT.Copy).then_inc(hi_ready, 1)

            def hi(base, s, use, to=None):
                act.wait_ge(mm_done, use + (s - 1))
                split(base, s, to)

            def x_squares(n, t):
                act.wait_ge(x_ready, n * TB + t + 1)
                act.activation(junk[:], xres[:, t, :], ACT.Square, accum_out=ss_x[:, t:t + 1]).then_inc(x_sq, 1)

            def h_parts(n, t):
                for half in range(2):
                    bank_t = (ps_t, ps_s)[half][:].rearrange("p (c n) -> p c n", c=KC // 2)
                    act.wait_ge(x_tr, n * 2 * TB + 2 * t + half + 1)
                    act.activation(h_hi[:, half * 4:half * 4 + 4, t * P:(t + 1) * P], bank_t, ACT.Copy)\
                        .then_inc(h_hi_ready, 1)

            x_squares(0, 0)
            split(0, 0)
            act.wait_ge(x_sq, 1)
            x_squares(0, 1)
            split(0, 1)
            h_parts(0, 0)
            act.wait_ge(x_sq, 2)
            x_squares(0, 2)
            h_parts(0, 1)

            with act.Fori(0, DEPTH) as l:
                def group(g, first_group):
                    base = l * LAYER_SLABS + g * GROUP_SLABS
                    use = l * LAYER_USES + g * GROUP_USES + 2
                    kg = l * KV_HEADS + g
                    for t in range(TB):
                        if first_group and t == 0:
                            act.wait_ge(x_sq, l * TB + 3)
                            x_squares(l, 3)
                            act.dma_start(residual.rearrange("(t p) n -> p t n", p=P), xres).then_inc(saved, 16)
                        act.wait_ge(mm_done, use + t + 1)
                        if t:
                            act.wait_ge(k_sq, kg * TB + t)
                        act.activation(k_junk, bank[t][:, 0:P], ACT.Square, accum_out=ss_k[:, t:t + 1])\
                            .then_inc(k_sq, 1)
                        act.activation(v_hi[:, t, :], bank[t][:, P:2 * P], ACT.Copy).then_inc(v_hi_ready, 1)
                        if first_group and t < 2:
                            h_parts(l, 2 + t)
                        if t == 1:
                            split(base + 2, 0, first_hi)
                        if t == TB - 1:
                            split(base + 2, 1)
                    if first_group:
                        act.wait_ge(par_ld, l * 16 + 16)

                    def unit(i, first):
                        base = l * LAYER_SLABS + g * GROUP_SLABS + i * UT + 2
                        use = l * LAYER_USES + g * GROUP_USES + i * UT + TB + 2
                        turns = l * LAYER_TURNS + g * (GROUP_USES // BANKS) + i * (UT // BANKS) + 1
                        u = l * HEADS + g * GROUP + i
                        j = g * GROUP + i
                        rope = kg * (GROUP + 1) + i + 1

                        def exps(t):
                            act.wait_ge(s_nb, u * TB + t + 1)
                            act.activation(probs[:, t, :], ps_s[:], ACT.Exp, bias=nb[:, t:t + 1],
                                           scale=srq[:, t:t + 1], accum_out=rs[:, t:t + 1]).then_inc(s_exp, 1)

                        def pt_part(t):
                            act.wait_ge(pt_tr, u * TB + t + 1)
                            if t >= 2:
                                act.wait_ge(pv_done, u * TB + t - 1)
                            act.activation(pt_hi[:, t % 2, :], ps_t[:], ACT.Copy).then_inc(pt_hi_ready, 1)

                        if first:
                            act.wait_ge(k_tr, kg + 1)
                            act.activation(g_hi[:], ps_t[:], ACT.Copy, scale=par[:, PC_GK:PC_GK + 1]).then_inc(g_hi_ready, 1)
                        hi(base, 2, use)
                        if first:
                            act.wait_ge(roped, rope)
                            act.activation(k_hi[:], rope1[:], ACT.Copy).then_inc(r_hi_ready, 1)
                        act.activation(g_hi[:], bank[0][:], ACT.Copy, scale=par[:, PC_GQ:PC_GQ + 1]).then_inc(g_hi_ready, 1)
                        act.activation(val[:], bank[0][:], ACT.Square).then_inc(q_sq, 1)
                        hi(base, 3, use)
                        act.activation(ac_sb[:], bank[1][:], ACT.Copy).then_inc(taken[1], 1)
                        act.wait_ge(roped, rope + 1)
                        act.activation(r_hi[:], rope1[:], ACT.Copy).then_inc(r_hi_ready, 1)
                        hi(base, 4, use)
                        exps(0)
                        exps(1)
                        hi(base, 5, use)
                        exps(2)
                        exps(3)
                        hi(base, 6, use)
                        act.activation(gate[:], bank[0][:], ACT.Tanh, scale=0.5).then_inc(a_tanh, 1)
                        pt_part(0)
                        hi(base, 7, use, last_hi[:])
                        pt_part(1)
                        act.wait_ge(taken[0], taken_at(turns, 4))
                        act.activation(gate[:], bank[1][:], ACT.Tanh, scale=0.5).then_inc(b_tanh, 1)
                        act.wait_ge(a_val, u + 1)
                        act.activation(p1_hi[:, j, :], val[:], ACT.Copy, scale=0.5).then_inc(a_hi, 1)
                        pt_part(2)
                        hi(base, 8, use)
                        act.wait_ge(taken[1], taken_at(turns, 5))
                        act.activation(gate[:], bank[2][:], ACT.Tanh, scale=0.5).then_inc(taken[2], 1)
                        pt_part(3)
                        hi(base, 9, use - 1)
                        act.wait_ge(b_val, u + 1)
                        act.activation(p2_hi[:, j, :], bval[:], ACT.Copy, scale=0.5).then_inc(b_hi, 1)

                    unit(0, True)
                    with act.Fori(1, GROUP) as i:
                        unit(i, False)

                group(0, True)
                with act.Fori(1, KV_HEADS) as g:
                    group(g, False)

                def gates(stage_slab, stage_use, squares=False, pairs=KC // 2):
                    with act.Fori(0, pairs) as jj:
                        base = l * LAYER_SLABS + stage_slab + jj * 4
                        use = l * LAYER_USES + stage_use + jj * 4 + 2
                        turns = l * LAYER_TURNS + stage_use // BANKS + jj
                        for s in range(2):
                            hi(base, 2 * s + 2, use)
                            act.wait_ge(taken[(2 * s + 3) % BANKS], taken_at(turns, 2 * s - 1))
                            act.activation(gate[:], bank[2 * s][:], ACT.Tanh, scale=0.5).then_inc(taken[2 * s], 1)
                            if squares:
                                act.wait_ge(ln_xc, l * KC + jj * 2 + s + 1)
                                act.wait_ge(ln_sum, l * (KC + 1) + jj * 2 + 1)
                                act.activation(sq[:, s, :], cc[:, jj * 2 + s + 1, :], ACT.Square).then_inc(ln_sq, 1)
                            hi(base, 2 * s + 3, use)

                gates(SLAB_A, USE_A)
                act.dma_start(gpost[:], post_gain[l].broadcast_to((P, D))).then_inc(post_ld, 16)
                act.dma_start(gpre[:], pre_gain[l + 1].broadcast_to((P, D))).then_inc(pre_ld, 16)
                gates(SLAB_B, USE_B, True)
                act.wait_ge(ln_var, l + 1)
                act.activation(val[:], ps_s[:], ACT.Sqrt, bias=ln_eps[:]).then_inc(ln_sd, 1)
                base = l * LAYER_SLABS + SLAB_G
                use = l * LAYER_USES + USE_G + 2
                for c in range(KC):
                    n = l * KC + c
                    act.wait_ge(n_n, n + 1)
                    if c:
                        act.wait_ge(n_s, n)
                    act.activation(ac_sb[:], cc[:, c + 1, :], ACT.Tanh, scale=0.5).then_inc(n_t, 1)
                    hi(base, c + 2, use)
                    if c:
                        act.wait_ge(taken[(c - 1) % BANKS], taken_at(l * LAYER_TURNS + USE_G // BANKS, c - 1))
                    act.activation(gate[:], bank[c % BANKS][:], ACT.Tanh, scale=0.5).then_inc(g_t, 1)
                    act.wait_ge(n_v, n + 1)
                    act.activation(p1_hi[:, c, :], bval[:], ACT.Copy, scale=0.25).then_inc(n_hi, 1)
                for t in range(TB):
                    act.dma_start(xres[:, t, :], residual[t * P:(t + 1) * P, :]).then_inc(xr_ld[t], 16)
                act.dma_start(par[:], params[l + 1]).then_inc(par_ld, 16)
                gates(SLAB_C, USE_C, pairs=KC // 2 - 1)
                base = l * LAYER_SLABS + SLAB_O
                use = l * LAYER_USES + USE_O + 2
                turns = l * LAYER_TURNS + USE_O // BANKS - 1
                for s in range(2):
                    if s == 0:
                        hi(base - 4, 2, use - 4)
                    else:
                        split(base, 0, o_hi[:, 0])
                        act.wait_ge(mm_done, use - 1)
                    act.wait_ge(taken[(2 * s + 3) % BANKS], taken_at(turns, 2 * s - 1))
                    act.activation(gate[:], bank[2 * s][:], ACT.Tanh, scale=0.5).then_inc(taken[2 * s], 1)
                    if s == 0:
                        hi(base - 4, 3, use - 4)
                split(base, 1, o_hi[:, 1])
                hi(base, 2, use - 2)
                hi(base, 3, use - 2)

                def o_squares(n, x_before):
                    t, half = O_ORDER[n]
                    act.wait_ge(mm_done, use + n + 1)
                    act.wait_ge(x_sq, l * TB + x_before)
                    if n:
                        act.wait_ge(o_sq, l * len(O_ORDER) + n)
                    act.activation(junk[:, 0:SEQ], bank[(2 * t + half) % BANKS][:], ACT.Square,
                                   accum_out=ss_o[:, t, half:half + 1]).then_inc(o_sq, 1)

                def next_squares(t, o_before):
                    act.wait_ge(o_sq, l * len(O_ORDER) + o_before)
                    act.wait_ge(x_sq, (l + 1) * TB + t)
                    x_squares(l + 1, t)

                split(base, 4, alt_hi[:, 0])
                split(base, 5, alt_hi[:, 1])
                o_squares(0, TB)
                split(base, 6, alt_hi[:, 2])
                o_squares(1, TB)
                split(base, 7, alt_hi[:, 3])
                o_squares(2, TB)
                o_squares(3, TB)
                next_squares(0, 4)
                next_squares(1, 4)
                o_squares(4, TB + 2)
                h_parts(l + 1, 0)
                o_squares(5, TB + 2)
                h_parts(l + 1, 1)
                next_squares(2, 6)
                o_squares(6, TB + 3)
                split((l + 1) * LAYER_SLABS, 0)
                split((l + 1) * LAYER_SLABS, 1)
                o_squares(7, TB + 3)
                act.wait_ge(o_sq, (l + 1) * len(O_ORDER))

        @block.tensor
        def _(pe):
            pe.wait_ge(setup, 6)
            pe.wait_ge(ident_ld, 16)

            def product(out, k, hi_a, lo_a, hi_b, lo_b, first, last):
                pe.matmul(out, hi_a, hi_b, start=first, stop=False)
                pe.matmul(out, hi_a, lo_b, start=False, stop=False)
                return pe.matmul(out, lo_a, hi_b, start=False, stop=last)

            def half_tile(slab, s, turns, b, act_hi, act_lo, part, ready=None, slab_hi=None, slab_lo=None):
                out = bank[b % BANKS][:]
                if slab_hi is None:
                    slab_hi, slab_lo = w_hi[:, s % 2], w_lo[:, s % 2]
                if part == 0:
                    pe.wait_ge(lo_ready, slab + s + 3)
                    pe.wait_ge(taken[b % BANKS], free_at(turns, b))
                if ready:
                    pe.wait_ge(*ready)
                for k in range(part * KC // 2, (part + 1) * KC // 2):
                    mm = product(out, k, slab_hi[:, k, :], slab_lo[:, k, :], act_hi[:, k, :], act_lo[:, k, :],
                                 k == 0, k == KC - 1)
                if part == 1:
                    mm.then_inc(mm_done, 1)

            def tile(slab, s, turns, b, act_hi=h_hi, act_lo=h_lo):
                half_tile(slab, s, turns, b, act_hi, act_lo, 0)
                half_tile(slab, s, turns, b, act_hi, act_lo, 1)

            def turn_x(n, t):
                pe.wait_ge(xn_ready, n * TB + t + 1)
                for half in range(2):
                    to = (ps_t, ps_s)[half]
                    if t:
                        pe.wait_ge(h_lo_ready, n * 2 * TB + 2 * t + half - 1)
                    for c in range(4):
                        mm = pe.transpose(to[:, c * P:(c + 1) * P], xn[t % 2][:, (half * 4 + c) * P:(half * 4 + c + 1) * P],
                                          ident_sb[:])
                    mm.then_inc(x_tr, 1)

            turn_x(0, 0)
            turn_x(0, 1)
            with pe.Fori(0, DEPTH) as l:
                def group(g, first_group):
                    kg = l * KV_HEADS + g
                    base = l * LAYER_SLABS + g * GROUP_SLABS
                    turns = l * LAYER_TURNS + g * (GROUP_USES // BANKS)
                    pe.wait_ge(lo_ready, base + 1 + 3)
                    for t in range(TB):
                        if first_group:
                            pe.wait_ge(h_lo_ready, l * 2 * TB + 2 * (t + 1))
                        pe.wait_ge(taken[t], free_at(turns, t))
                        ts = slice(t * P, (t + 1) * P)
                        for k in range(KC):
                            mm = product(bank[t][:, 0:2 * P], k, h_hi[:, k, ts], h_lo[:, k, ts], w_hi[:, :, k, :],
                                         w_lo[:, :, k, :], k == 0, k == KC - 1)
                        mm.then_inc(mm_done, 1)
                        if first_group and t < 2:
                            turn_x(l, 2 + t)

                    def rotate(n):
                        pe.wait_ge(rot_ready, 1)
                        pe.wait_ge(g_lo_ready, n)
                        pe.matmul(ps_t[:], rot_r[:], g_hi[:], start=True, stop=False)
                        pe.matmul(ps_t[:], rot_r[:], g_lo[:], start=False, stop=True).then_inc(rot_done, 1)

                    def unit(i, first):
                        base = l * LAYER_SLABS + g * GROUP_SLABS + i * UT + 2
                        turns = l * LAYER_TURNS + g * (GROUP_USES // BANKS) + i * (UT // BANKS) + 1
                        u = l * HEADS + g * GROUP + i
                        rope = kg * (GROUP + 1) + i + 1

                        def part(s, n):
                            own = (first_hi, first_lo) if first and s == 0 else (last_hi, last_lo) if s == UT - 1 else (None, None)
                            half_tile(base, s, turns, s, h_hi, h_lo, n, None, *own)

                        def scores(t):
                            pe.wait_ge(r_lo_ready, rope + 1)
                            ts = slice(t * P, (t + 1) * P)
                            if t == 0:
                                pe.wait_ge(q_ms, u + 1)
                            else:
                                pe.wait_ge(s_exp, u * TB + t)
                            product(ps_s[:], 0, r_hi[:, ts], r_lo[:, ts], k_hi[:], k_lo[:], True, True).then_inc(s_done, 1)

                        def turn(b):
                            if b == 0:
                                pe.wait_ge(p_ready, u * TB + TB)
                            else:
                                pe.wait_ge(pt_lo_ready, u * TB + b)
                            for t in range(TB):
                                mm = pe.transpose(ps_t[:, t * P:(t + 1) * P], probs[:, t, b * P:(b + 1) * P], ident_sb[:])
                            mm.then_inc(pt_tr, 1)

                        def pv(b):
                            pe.wait_ge(pt_lo_ready, u * TB + b + 1)
                            product(ps_o[:], b, v_hi[:, b, :], v_lo[:, b, :], pt_hi[:, b % 2, :], pt_lo[:, b % 2, :],
                                    b == 0, b == TB - 1).then_inc(pv_done, 1)

                        part(0, 0)
                        part(0, 1)
                        if first:
                            pe.wait_ge(k_norm, kg + 1)
                            for t in range(TB):
                                mm = pe.transpose(ps_t[:, t * P:(t + 1) * P], k_raw[:, t, :], ident_sb[:])
                            mm.then_inc(k_tr, 1)
                        part(1, 0)
                        if first:
                            pe.wait_ge(rope1_ready, kg + 1)
                            rotate(rope)
                            part(1, 1)
                            part(2, 0)
                        pe.wait_ge(q_sq, u + 1)
                        for t in range(TB):
                            mm = pe.matmul(ps_s[:, t:t + 1], val[:, t * P:(t + 1) * P], ones[:], start=True, stop=True)
                        mm.then_inc(q_ss, 1)
                        if not first:
                            part(1, 1)
                        rotate(rope + 1)
                        if not first:
                            part(2, 0)
                        part(2, 1)
                        scores(0)
                        part(3, 0)
                        scores(1)
                        part(3, 1)
                        scores(2)
                        part(4, 0)
                        scores(3)
                        part(4, 1)
                        part(5, 0)
                        turn(0)
                        part(5, 1)
                        turn(1)
                        pv(0)
                        part(6, 0)
                        turn(2)
                        pv(1)
                        part(6, 1)
                        turn(3)
                        pv(2)
                        part(7, 0)
                        pv(3)
                        part(7, 1)

                    unit(0, True)
                    with pe.Fori(1, GROUP) as i:
                        unit(i, False)

                group(0, True)
                with pe.Fori(1, KV_HEADS) as g:
                    group(g, False)

                def projection(slab_at, use_at, ready, value, in_hi, in_lo):
                    with pe.Fori(0, KC // 2) as jj:
                        base = l * LAYER_SLABS + slab_at + jj * 4
                        turns = l * LAYER_TURNS + use_at // BANKS + jj
                        for s in range(2):
                            tile(base, 2 * s, turns, 2 * s)
                            half_tile(base, 2 * s + 1, turns, 2 * s + 1, in_hi, in_lo, 0, (ready, value - KC // 2))
                            half_tile(base, 2 * s + 1, turns, 2 * s + 1, in_hi, in_lo, 1, (ready, value))

                projection(SLAB_A, USE_A, a_lo, l * KC + KC, p1_hi, p1_lo)
                pe.wait_ge(c_summed, (l + 1) * (KC + 1))
                pe.matmul(ps_o[:], mean_w[:], c_sum, start=True, stop=True).then_inc(ln_mean, 1)
                projection(SLAB_B, USE_B, b_lo, l * KC + KC, p2_hi, p2_lo)
                pe.wait_ge(ln_sum, (l + 1) * (KC + 1))
                pe.matmul(ps_s[:], mean_w[:], c_sum, start=True, stop=True).then_inc(ln_var, 1)
                with pe.Fori(0, 2) as jj:
                    for c in range(KC // 2):
                        tile(l * LAYER_SLABS + SLAB_G + jj * 4, c, l * LAYER_TURNS + USE_G // BANKS + jj, c)
                projection(SLAB_C, USE_C, n_lo, l * KC + KC, p1_hi, p1_lo)
                base = l * LAYER_SLABS + SLAB_O
                turns = l * LAYER_TURNS + USE_O // BANKS
                o_pairs = ((o_hi, o_lo), (w_hi, w_lo), (alt_hi[:, 0:2], alt_lo[:, 0:2]), (alt_hi[:, 2:4], alt_lo[:, 2:4]))

                def o_product(t, pair, chunks=range(KC), first_time=False):
                    b = 2 * t + pair // 2
                    to = bank[b % BANKS][:, pair % 2 * 2 * P:(pair % 2 + 1) * 2 * P]
                    ts = slice(t * P, (t + 1) * P)
                    pair_hi, pair_lo = o_pairs[pair]
                    if chunks[0] == 0:
                        pe.wait_ge(lo_ready, base + 2 * pair + 1 + 3)
                        if pair % 2 == 0:
                            pe.wait_ge(taken[b % BANKS], free_at(turns, b))
                    for k in chunks:
                        if first_time:
                            pe.wait_ge(y_lo, l * KC + k + 1)
                        mm = product(to, k, p2_hi[:, k, ts], p2_lo[:, k, ts], pair_hi[:, :, k, :], pair_lo[:, :, k, :],
                                     k == 0, k == KC - 1)
                    if pair % 2 == 1:
                        mm.then_inc(mm_done, 1)

                o_product(0, 0, range(KC - 1), True)
                o_product(1, 0, range(KC - 1))
                o_product(0, 0, range(KC - 1, KC), True)
                o_product(1, 0, range(KC - 1, KC))
                for pair in range(1, 4):
                    o_product(0, pair)
                    o_product(1, pair)
                for t in (2, 3):
                    for half in range(HALVES):
                        o_product(t, 2 * half)
                        o_product(t, 2 * half + 1)
                        if t == 2:
                            turn_x(l + 1, half)

        @block.vector
        def _(dve):
            dve.wait_ge(setup, 6)
            for t in range(TB):
                dve.wait_ge(xr_ld[t], 16)
                dve.memset(ri[:, t:t + 1], 0.0).then_inc(x_ready, 1)

            def minus(out, full, scale, hi_part, done):
                return dve.scalar_tensor_tensor(out, full, scale, hi_part.bitcast(F32), ALU.mult, ALU.subtract)\
                    .then_inc(done, 1)

            def conv_c(n, chunk, turns):
                first = n * TAPS_C
                dve.tensor_scalar(ctap[:], par[:, PC_C:PC_C + (KC + 1) * TAPS_C]
                                  .rearrange("p (c t) -> p c t", t=TAPS_C)[:, chunk, :], 0.5, None, ALU.mult)\
                    .then_inc(taps_ready, 1)
                dve.tensor_scalar(cbias[:], par[:, bass.ds(chunk + PC_BIAS, 1)], 1.0, None, ALU.mult)\
                    .then_inc(taps_ready, 1)
                for m in range(TAPS_C):
                    source = upad[:, m:m + SEQ]
                    w = ctap[:, m:m + 1]
                    if m == 0:
                        dve.wait_ge(taken[BANKS - 1], free_at(turns, 0))
                        dve.wait_ge(taps_ready, n * 2 + 2)
                        dve.wait_ge(c_ready, n + 1)
                        dve.tensor_scalar(ps_c[:], source, w, cbias[:], ALU.mult, ALU.add).then_inc(c_step, 1)
                    elif m == 1:
                        dve.tensor_scalar(acc1[:], source, w, None, ALU.mult).then_inc(c_step, 1)
                    else:
                        to = (ps_c if m % 2 == 0 else acc1)[:]
                        dve.wait_ge(c_step, first + m - 1)
                        dve.scalar_tensor_tensor(to, source, w, to, ALU.mult, ALU.add).then_inc(c_step, 1)
                    yield
                dve.wait_ge(c_step, first + TAPS_C)
                dve.tensor_tensor(cc[:, chunk, :], ps_c[:], acc1[:], ALU.add).then_inc(c_ready, 1)
                dve.wait_ge(c_ready, n + 2)
                dve.tensor_tensor(c_sum, c_sum, cc[:, chunk, :], ALU.add).then_inc(c_summed, 1)

            def normed(n, t):
                dve.wait_ge(x_sq, n * TB + t + 1)
                dve.tensor_scalar(ms_x[:, t:t + 1], ss_x[:, t:t + 1], 1.0 / D, RMS_EPS, ALU.mult, ALU.add).then_inc(x_ms, 1)
                if t == 0:
                    dve.wait_ge(pre_ld, n * 16 + 16)
                dve.wait_ge(x_r, n * TB + t + 1)
                if t >= 2:
                    dve.wait_ge(x_tr, n * 2 * TB + 2 * (t - 1))
                dve.scalar_tensor_tensor(xn[t % 2][:], xres[:, t, :], rx[:, t:t + 1], gpre[:], ALU.mult, ALU.mult)\
                    .then_inc(xn_ready, 1)

            def h_rests(n, t):
                for half in range(2):
                    bank_t = (ps_t, ps_s)[half][:].rearrange("p (c n) -> p c n", c=KC // 2)
                    dve.wait_ge(h_hi_ready, n * 2 * TB + 2 * t + half + 1)
                    dve.tensor_tensor(h_lo[:, half * 4:half * 4 + 4, t * P:(t + 1) * P], bank_t,
                                      h_hi[:, half * 4:half * 4 + 4, t * P:(t + 1) * P].bitcast(F32), ALU.subtract)\
                        .then_inc(h_lo_ready, 1)

            normed(0, 0)
            normed(0, 1)
            h_rests(0, 0)
            normed(0, 2)
            h_rests(0, 1)
            with dve.Fori(0, DEPTH) as l:
                def group(g, first_group):
                    kg = l * KV_HEADS + g
                    for t in range(TB):
                        if first_group and t == 0:
                            normed(l, 3)
                        dve.wait_ge(v_hi_ready, kg * TB + t + 1)
                        dve.wait_ge(k_sq, kg * TB + t + 1)
                        dve.tensor_copy(k_raw[:, t, :], bank[t][:, 0:P]).then_inc(k_copied, 1)
                        dve.tensor_tensor(v_lo[:, t, :], bank[t][:, P:2 * P], v_hi[:, t, :].bitcast(F32), ALU.subtract)\
                            .then_inc(taken[t], 1)
                        if first_group and t < 2:
                            h_rests(l, 2 + t)
                    if first_group:
                        dve.wait_ge(const_ld, 2 * 16)
                        dve.wait_ge(saved, l * 16 + 16)
                    dve.tensor_scalar(ms_k[:], ss_k[:], 1.0 / P, RMS_EPS, ALU.mult, ALU.add).then_inc(k_ms, 1)
                    dve.wait_ge(k_r, kg + 1)
                    dve.wait_ge(k_copied, kg * TB + TB)
                    for t in range(TB):
                        k_scaled = dve.tensor_scalar(k_raw[:, t, :], k_raw[:, t, :], rk[:, t:t + 1], None, ALU.mult)
                    k_scaled.then_inc(k_norm, 1)

                    def rope(source, gain, n, squared, done):
                        dve.wait_ge(g_hi_ready, n)
                        if squared is not None:
                            dve.wait_ge(q_sq, squared)
                            dve.wait_ge(r_lo_ready, n - 1)
                        minus(g_lo[:], source, gain, g_hi[:], g_lo_ready)
                        dve.scalar_tensor_tensor(rope1[:], source, gain, cos_sb[:], ALU.mult, ALU.mult).then_inc(done, 1)

                    def rope_end(n, one, value, lo_to, hi_to):
                        dve.wait_ge(rot_done, n)
                        dve.tensor_tensor(rope2[:], ps_t[:], sin_sb[:], ALU.mult).then_inc(rope2_ready, 1)
                        dve.wait_ge(rope2_ready, n)
                        dve.wait_ge(one, value)
                        dve.tensor_tensor(rope1[:], rope1[:], rope2[:], ALU.add).then_inc(roped, 1)
                        dve.wait_ge(r_hi_ready, n)
                        dve.wait_ge(roped, n)
                        dve.tensor_tensor(lo_to[:], rope1[:], hi_to[:].bitcast(F32), ALU.subtract).then_inc(r_lo_ready, 1)

                    def unit(i, first):
                        use = l * LAYER_USES + g * GROUP_USES + i * UT + TB + 2
                        turns = l * LAYER_TURNS + g * (GROUP_USES // BANKS) + i * (UT // BANKS) + 1
                        u = l * HEADS + g * GROUP + i
                        j = g * GROUP + i
                        n_rope = kg * (GROUP + 1) + i + 2
                        conv = conv_c(l * (KC + 1) + j, j, turns)

                        def taps(n):
                            for _ in range(n):
                                next(conv, None)

                        def softmax_max(t):
                            dve.wait_ge(s_done, u * TB + t + 1)
                            dve.tensor_reduce(mx[:, t:t + 1], ps_s[:], AX_X, ALU.max).then_inc(s_max, 1)
                            if t == 0:
                                dve.wait_ge(q_r, u + 1)
                                dve.tensor_scalar(srq[:], rq[:], SCALE, None, ALU.mult).then_inc(q_sr, 1)
                                dve.wait_ge(q_sr, u + 1)
                            dve.wait_ge(s_max, u * TB + t + 1)
                            dve.tensor_scalar(nb[:, t:t + 1], mx[:, t:t + 1], srq[:, t:t + 1], -1.0, ALU.mult, ALU.mult)\
                                .then_inc(s_nb, 1)

                        def softmax_end(t):
                            dve.wait_ge(s_exp, u * TB + t + 1)
                            dve.reciprocal(ri[:, t:t + 1], rs[:, t:t + 1]).then_inc(s_ri, 1)
                            dve.wait_ge(s_ri, u * TB + t + 1)
                            dve.tensor_scalar(probs[:, t, :], probs[:, t, :], ri[:, t:t + 1], None, ALU.mult).then_inc(p_ready, 1)

                        def pt_rest(t):
                            dve.wait_ge(pt_hi_ready, u * TB + t + 1)
                            dve.tensor_tensor(pt_lo[:, t % 2, :], ps_t[:], pt_hi[:, t % 2, :].bitcast(F32), ALU.subtract)\
                                .then_inc(pt_lo_ready, 1)

                        if first:
                            dve.wait_ge(k_tr, kg + 1)
                            rope(ps_t[:], par[:, PC_GK:PC_GK + 1], n_rope - 1, None, rope1_ready)
                        taps(2)
                        if first:
                            rope_end(n_rope - 1, rope1_ready, kg + 1, k_lo, k_hi)
                        rope(bank[0][:], par[:, PC_GQ:PC_GQ + 1], n_rope, u + 1, taken[0])
                        taps(2)
                        dve.wait_ge(q_ss, u + 1)
                        dve.tensor_scalar(ms_q[:], ps_s[:, 0:TB], 1.0 / P, RMS_EPS, ALU.mult, ALU.add).then_inc(q_ms, 1)
                        taps(2)
                        rope_end(n_rope, taken[0], taken_at(turns, 0), r_lo, r_hi)
                        dve.tensor_scalar(atap[:], par[:, PC_A:PC_A + KC * TAPS_A]
                                          .rearrange("p (c t) -> p c t", t=TAPS_A)[:, j, :], 1.0, None, ALU.mult)\
                            .then_inc(a_conv, 1)
                        taps(3)
                        softmax_max(0)
                        dve.wait_ge(mm_done, use + 3)
                        dve.wait_ge(taken[1], taken_at(turns, 1))
                        dve.tensor_tensor(axpad[:, PAD_A:PAD_A + SEQ], bank[2][:], ac_sb[:], ALU.mult)\
                            .then_inc(taken[2], 1)
                        taps(2)
                        softmax_max(1)
                        softmax_end(0)
                        taps(1)
                        dve.wait_ge(taken[2], taken_at(turns, 2))
                        dve.wait_ge(a_conv, u * 4 + 1)
                        dve.tensor_scalar(ca[:, 0, :], axpad[:, 0:SEQ], atap[:, 0:1], None, ALU.mult).then_inc(a_conv, 1)
                        taps(1)
                        softmax_max(2)
                        softmax_end(1)
                        for m in (1, 2):
                            dve.wait_ge(a_conv, u * 4 + m + 1)
                            dve.scalar_tensor_tensor(ca[:, 0, :], axpad[:, m:m + SEQ], atap[:, m:m + 1], ca[:, 0, :],
                                                     ALU.mult, ALU.add).then_inc(a_conv, 1)
                            taps(1)
                        softmax_max(3)
                        softmax_end(2)
                        dve.wait_ge(mm_done, use + 4)
                        dve.wait_ge(a_conv, u * 4 + 4)
                        dve.tensor_tensor(ca[:, 0, :], ca[:, 0, :], bank[3][:], ALU.mult)\
                            .then_inc(taken[3], 1)
                        taps(1)
                        softmax_end(3)
                        taps(3)
                        pt_rest(0)
                        dve.wait_ge(a_tanh, u + 1)
                        dve.scalar_tensor_tensor(ca[:, 1, :], gate[:], 1.0, bank[0][:], ALU.add, ALU.mult)\
                            .then_inc(taken[0], 1)
                        taps(1)
                        pt_rest(1)
                        dve.wait_ge(taken[0], taken_at(turns, 4))
                        dve.wait_ge(taken[3], taken_at(turns, 3))
                        dve.tensor_tensor(val[:], ca[:, 0, :], ca[:, 1, :], ALU.mult).then_inc(a_val, 1)
                        taps(3)
                        pt_rest(2)
                        dve.wait_ge(a_hi, u + 1)
                        minus(p1_lo[:, j, :], val[:], 0.5, p1_hi[:, j, :], a_lo)
                        dve.wait_ge(b_tanh, u + 1)
                        dve.scalar_tensor_tensor(ca[:, 1, :], gate[:], 1.0, bank[1][:], ALU.add, ALU.mult)\
                            .then_inc(taken[1], 1)
                        taps(3)
                        pt_rest(3)
                        taps(TAPS_C)
                        dve.wait_ge(pv_done, u * TB + TB)
                        dve.wait_ge(taken[1], taken_at(turns, 5))
                        dve.tensor_tensor(bval[:], ps_o[:], ca[:, 1, :], ALU.mult).then_inc(b_val, 1)
                        dve.wait_ge(b_hi, u + 1)
                        minus(p2_lo[:, j, :], bval[:], 0.5, p2_hi[:, j, :], b_lo)
                        dve.wait_ge(taken[2], taken_at(turns, 6))
                        dve.wait_ge(mm_done, use + 8)
                        dve.scalar_tensor_tensor(upad[:, PAD_C:PAD_C + SEQ], gate[:], 1.0, bank[3][:], ALU.add, ALU.mult)\
                            .then_inc(taken[3], 1)

                    unit(0, True)
                    with dve.Fori(1, GROUP) as i:
                        unit(i, False)
                group(0, True)
                with dve.Fori(1, KV_HEADS) as g:
                    group(g, False)

                def merged(use_at, n, conv=None):
                    def two_chunks(jj):
                        use = l * LAYER_USES + use_at + jj * 4 + 2
                        turns = l * LAYER_TURNS + use_at // BANKS + jj
                        for s in range(2):
                            j = jj * 2 + s
                            if n == 1:
                                dve.tensor_tensor(cc[:, j + 1, :], cc[:, j + 1, :], ps_o[:], ALU.subtract).then_inc(ln_xc, 1)
                            dve.wait_ge(taken[2 * s], taken_at(turns, 2 * s))
                            dve.wait_ge(mm_done, use + 2 * s + 2)
                            to = y[:, j, :] if n == 0 else bval[:]
                            dve.scalar_tensor_tensor(to, gate[:], 1.0, bank[2 * s + 1][:], ALU.add, ALU.mult)\
                                .then_inc(taken[2 * s + 1], 1)
                            if n == 1:
                                dve.wait_ge(ln_sq, l * KC + jj * 2 + s + 1)
                                dve.wait_ge(ln_sum, l * (KC + 1) + jj * 2 + s + 1)
                                dve.tensor_tensor(c_sum, c_sum, sq[:, s, :], ALU.add).then_inc(ln_sum, 1)
                            if n:
                                dve.wait_ge(taken[2 * s + 1], taken_at(turns, 2 * s + 1))
                                dve.tensor_tensor(y[:, j, :], y[:, j, :], bval[:], ALU.add).then_inc(y_ready, 1)
                                dve.wait_ge(y_ready, l * 2 * KC + (n - 1) * KC + jj * 2 + s + 1)
                            if n == 2:
                                dve.tensor_scalar(p2_hi[:, j, :], y[:, j, :], 0.5, None, ALU.mult).then_inc(y_hi, 1)
                                dve.wait_ge(y_hi, l * KC + jj * 2 + s + 1)
                                minus(p2_lo[:, j, :], y[:, j, :], 0.5, p2_hi[:, j, :], y_lo)
                            for _ in range(TAPS_C // (KC // 2) + 1 if conv else 0):
                                next(conv, None)

                    if conv:
                        for jj in range(KC // 2):
                            two_chunks(jj)
                    else:
                        with dve.Fori(0, KC // 2) as jj:
                            two_chunks(jj)

                merged(USE_A, 0, conv_c(l * (KC + 1) + KC, KC, l * LAYER_TURNS + USE_A // BANKS))
                dve.wait_ge(ln_mean, l + 1)
                dve.memset(c_sum, 0.0).then_inc(ln_sum, 1)
                merged(USE_B, 1)
                dve.wait_ge(ln_sd, l + 1)
                dve.reciprocal(acc1[:], val[:]).then_inc(ln_r, 1)
                dve.wait_ge(ln_r, l + 1)
                dve.wait_ge(ln_xc, l * KC + KC)

                def layer_normed(c):
                    n = l * KC + c
                    dve.tensor_tensor(cc[:, c + 1, :], cc[:, c + 1, :], acc1[:], ALU.mult).then_inc(n_z, 1)
                    dve.wait_ge(n_z, n + 1)
                    dve.tensor_scalar(cc[:, c + 1, :], cc[:, c + 1, :], par[:, PC_LNG + c:PC_LNG + c + 1],
                                      par[:, PC_LNB + c:PC_LNB + c + 1], ALU.mult, ALU.add).then_inc(n_n, 1)

                layer_normed(0)
                for c in range(KC):
                    n = l * KC + c
                    dve.wait_ge(n_n, n + 1)
                    dve.wait_ge(n_t, n + 1)
                    dve.scalar_tensor_tensor(ca[:, 0, :], ac_sb[:], 1.0, cc[:, c + 1, :], ALU.add, ALU.mult).then_inc(n_s, 1)
                    if c + 1 < KC:
                        layer_normed(c + 1)
                    dve.wait_ge(g_t, n + 1)
                    dve.scalar_tensor_tensor(val[:], gate[:], 1.0, bank[c % BANKS][:], ALU.add, ALU.mult)\
                        .then_inc(taken[c % BANKS], 1)
                    dve.wait_ge(n_s, n + 1)
                    dve.wait_ge(taken[c % BANKS], taken_at(l * LAYER_TURNS + USE_G // BANKS, c))
                    dve.tensor_tensor(bval[:], val[:], ca[:, 0, :], ALU.mult).then_inc(n_v, 1)
                    dve.wait_ge(n_hi, n + 1)
                    dve.wait_ge(n_v, n + 1)
                    minus(p1_lo[:, c, :], bval[:], 0.25, p1_hi[:, c, :], n_lo)
                merged(USE_C, 2)

                def half_square(t):
                    dve.wait_ge(o_sq, l * len(O_ORDER) + O_ORDER.index((t, 0)) + 1)
                    dve.tensor_scalar(half_ms[:, t:t + 1], ss_o[:, t, 0:1], 1.0 / D, RMS_EPS, ALU.mult, ALU.add)\
                        .then_inc(o_half, 1)

                def finished(t):
                    n = l * TB + t + 1
                    dve.wait_ge(o_sq, l * len(O_ORDER) + O_ORDER.index((t, 1)) + 1)
                    dve.wait_ge(o_half, n)
                    dve.tensor_scalar(ms_o[:, t:t + 1], ss_o[:, t, 1:2], 1.0 / D, half_ms[:, t:t + 1], ALU.mult, ALU.add)\
                        .then_inc(o_ms, 1)
                    if t == 0:
                        dve.wait_ge(post_ld, l * 16 + 16)
                    dve.wait_ge(xr_ld[t], l * 16 + 32)
                    dve.wait_ge(o_r, n)
                    for half in range(HALVES):
                        b = 2 * t + half
                        cols = slice(half * SEQ, (half + 1) * SEQ)
                        dve.scalar_tensor_tensor(yo[:, t % 2, cols], bank[b % BANKS][:], ro[:, t:t + 1], gpost[:, cols],
                                                 ALU.mult, ALU.mult).then_inc(taken[b % BANKS], 1)
                    for half in range(HALVES):
                        b = 2 * t + half
                        dve.wait_ge(taken[b % BANKS], taken_at(l * LAYER_TURNS + USE_O // BANKS, b))
                    dve.tensor_tensor(xres[:, t, :], xres[:, t, :], yo[:, t % 2, :], ALU.add).then_inc(x_ready, 1)

                half_square(0)
                half_square(1)
                finished(0)
                finished(1)
                normed(l + 1, 0)
                normed(l + 1, 1)
                half_square(2)
                h_rests(l + 1, 0)
                finished(2)
                h_rests(l + 1, 1)
                normed(l + 1, 2)
                half_square(3)
                finished(3)


def rope_tables():
    n_freq = P // 4
    inv_freq = (np.float32(THETA) ** (-np.arange(n_freq, dtype=np.float32) / np.float32(n_freq))).astype(np.float32)
    tokens = np.arange(SEQ)
    pos = np.stack([tokens // GRID_W, tokens % GRID_W]).astype(np.float32)
    angle = (inv_freq[None, :, None] * pos[:, None, :]).astype(np.float32)
    angle = np.repeat(angle[:, None], 2, axis=1).reshape(P, SEQ)
    return np.cos(angle).astype(np.float32), np.sin(angle).astype(np.float32)


def rotation():
    quarter = P // 4
    r = np.zeros((P, P), np.float32)
    for m in range(P):
        if m // quarter % 2 == 0:
            r[m + quarter, m] = -1.0
        else:
            r[m - quarter, m] = 1.0
    return r


def kernel(**inputs):
    import concourse.bacc as bacc
    from concourse.bass_utils import run_bass_kernel_spmd

    a = {k: np.asarray(v) for k, v in inputs.items()}
    f32 = np.float32

    blocks = {n: a[n].reshape(DEPTH, KC, P, -1, P) for n in ("w_in", "w_out_a", "w_out_b", "w_out_c", "w_o")}
    order = slab_order()
    slabs = np.zeros((DEPTH * LAYER_SLABS // 2 + 1, 2, P, KC, P), f32)
    flat = slabs[:-1].reshape(DEPTH, LAYER_SLABS, P, KC, P)
    for n, (name, b) in enumerate(order):
        flat[:, n] = blocks[name][:, :, :, b, :].transpose(0, 2, 1, 3)

    params = np.zeros((DEPTH + 1, P, PC_N), f32)
    by_chunk = lambda v: v.reshape(DEPTH, -1, KC, P).transpose(0, 3, 2, 1)
    params[:DEPTH, :, PC_C + TAPS_C:PC_BIAS] = by_chunk(a["conv_c_w"]).reshape(DEPTH, P, -1)
    params[:DEPTH, :, PC_BIAS + 1:PC_A] = by_chunk(a["conv_c_b"])[..., 0]
    params[:DEPTH, :, PC_A:PC_LNG] = by_chunk(a["conv_a_w"]).reshape(DEPTH, P, -1)
    params[:DEPTH, :, PC_LNG:PC_LNB] = by_chunk(a["ln_c_g"])[..., 0]
    params[:DEPTH, :, PC_LNB:PC_GQ] = by_chunk(a["ln_c_b"])[..., 0]
    params[:DEPTH, :, PC_GQ] = a["q_norm"]
    params[:DEPTH, :, PC_GK] = a["k_norm"]
    pre = np.concatenate([a["norm_pre"], np.zeros((1, D), f32)])
    cos, sin = rope_tables()
    arrays = {
        "x": a["x"].reshape(SEQ, D), "slabs": slabs, "params": params, "pre_gain": pre.reshape(DEPTH + 1, 1, D),
        "post_gain": a["norm_post"].reshape(DEPTH, 1, D), "ident": np.eye(P, dtype=f32), "rot": rotation(), "cos": cos, "sin": sin,
    }
    nc = bacc.Bacc("TRN2", target_bir_lowering=False, num_devices=1)
    args = [nc.dram_tensor(n, v.shape, F32, kind="ExternalInput").ap() for n, v in arrays.items()]
    residual = nc.dram_tensor("residual", (SEQ, D), F32).ap()
    out = nc.dram_tensor("out", (SEQ, D), F32, kind="ExternalOutput").ap()
    encoder_kernel(nc, *args, residual, out)
    r = run_bass_kernel_spmd(nc, [arrays], core_ids=[0])
    return np.asarray(r.results[0]["out"]).reshape(1, SEQ, D)
```
